# Optimizing a Trainium2 kernel written in Bass

```python
import jax, jax.numpy as jnp
from jax import lax
import numpy as np
import math

D_MODEL = 1024
BATCH = 1
SEQ = 256
DEPTH = 2

N_MEM = 256
GLA_HEADS = 6
GLA_DK = 64
GLA_DV = 128
GLA_K = GLA_HEADS * GLA_DK
GLA_V = GLA_HEADS * GLA_DV
GLA_GATE_RANK = 16
GLA_TAU = 16.0
GLA_CHUNK = 64
SB_HEADS = 12
SB_DIM = 64
SB_W = SB_HEADS * SB_DIM
SB_BLOCK = 128
MEM_HEADS = 4
MEM_DIM = 64
MEM_W = MEM_HEADS * MEM_DIM
PEER_HEADS = 8
PEER_KEYS = 128
PEER_EXPERTS = PEER_KEYS * PEER_KEYS
PEER_TOPK = 16
PEER_QHALF = 128
PEER_TOKEN_BLOCK = 128
N_A_LAYERS = DEPTH // 2
N_B_LAYERS = DEPTH - N_A_LAYERS
DEEPNORM_ALPHA = (2.0 * DEPTH) ** 0.25
DEEPNORM_BETA = (8.0 * DEPTH) ** -0.25
EPS = 1e-5
A_IN_SPLITS = [GLA_K, 2 * GLA_K, 2 * GLA_K + GLA_V, 2 * GLA_K + 2 * GLA_V, 2 * GLA_K + 2 * GLA_V + GLA_GATE_RANK]
A_IN_W = 2 * GLA_K + 2 * GLA_V + GLA_GATE_RANK + MEM_W
B_IN_W = SB_W + MEM_W


def layer_norm(x, g, b):
    xf = x.astype(jnp.float32)
    mu = jnp.mean(xf, axis=-1, keepdims=True)
    var = jnp.mean(jnp.square(xf - mu), axis=-1, keepdims=True)
    return ((xf - mu) * lax.rsqrt(var + EPS) * g + b).astype(x.dtype)

def to_heads(t, n_heads, d):
    B, T, _ = t.shape
    return t.reshape(B, T, n_heads, d).transpose(0, 2, 1, 3)

def from_heads(t):
    B, H, T, d = t.shape
    return t.transpose(0, 2, 1, 3).reshape(B, T, H * d)

def memory_attention(qm, mem, w_mem_kv):
    B, T, _ = qm.shape
    kv = mem @ w_mem_kv
    km, vm = jnp.split(kv, [MEM_W], axis=-1)
    q = qm.reshape(B, T, MEM_HEADS, MEM_DIM)
    k = km.reshape(B, -1, MEM_HEADS, MEM_DIM)
    v = vm.reshape(B, -1, MEM_HEADS, MEM_DIM)
    s = jnp.einsum('bthd,bmhd->bhtm', q, k).astype(jnp.float32) * (MEM_DIM ** -0.5)
    p = jax.nn.softmax(s, axis=-1).astype(v.dtype)
    return jnp.einsum('bhtm,bmhd->bthd', p, v).reshape(B, T, MEM_W)

def gla_chunked(q, k, v, log_g):
    B, H, T, dk = q.shape
    dv = v.shape[-1]
    n = T // GLA_CHUNK
    c = lambda t: t.astype(jnp.float32).reshape(B, H, n, GLA_CHUNK, t.shape[-1])
    q, k, v, log_g = c(q), c(k), c(v), c(log_g)
    b = jnp.cumsum(log_g, axis=-2)
    b_last = b[..., -1, :]
    q_dec = q * jnp.exp(b)
    k_inv = k * jnp.exp(-b)
    causal = jnp.tril(jnp.ones((GLA_CHUNK, GLA_CHUNK), dtype=bool))
    attn = jnp.where(causal, jnp.einsum('bhncd,bhnsd->bhncs', q_dec, k_inv), 0.0)
    o_intra = jnp.einsum('bhncs,bhnsv->bhncv', attn, v)
    k_to_end = k * jnp.exp(b_last[..., None, :] - b)
    du = jnp.einsum('bhncd,bhncv->bhndv', k_to_end, v)

    def step(S, inp):
        decay, inc = inp
        return decay[..., None] * S + inc, S

    S0 = jnp.zeros((B, H, dk, dv), jnp.float32)
    _, S_start = lax.scan(step, S0, (jnp.moveaxis(jnp.exp(b_last), 2, 0), jnp.moveaxis(du, 2, 0)))
    S_start = jnp.moveaxis(S_start, 0, 2)
    o_inter = jnp.einsum('bhncd,bhndv->bhncv', q_dec, S_start)
    return (o_intra + o_inter).reshape(B, H, T, dv)

def gla_layer_mixer(x, mem, w_in, w_gate2, b_gate, head_g, w_mem_kv, w_out):
    proj = x @ w_in
    q, k, v, r, glr, qm = jnp.split(proj, A_IN_SPLITS, axis=-1)
    log_g = jax.nn.log_sigmoid((glr @ w_gate2 + b_gate).astype(jnp.float32)) / GLA_TAU
    o = gla_chunked(to_heads(q, GLA_HEADS, GLA_DK) * (GLA_DK ** -0.5),
                    to_heads(k, GLA_HEADS, GLA_DK),
                    to_heads(v, GLA_HEADS, GLA_DV),
                    to_heads(log_g, GLA_HEADS, GLA_DK))
    o = o * lax.rsqrt(jnp.mean(jnp.square(o), axis=-1, keepdims=True) + EPS) * head_g[None, :, None, :]
    o = from_heads(o).astype(x.dtype) * jax.nn.silu(r)
    m = memory_attention(qm, mem, w_mem_kv)
    return jnp.concatenate([o, m], axis=-1) @ w_out

def stick_breaking(q, k, v):
    B, H, T, d = q.shape
    scale = d ** -0.5
    outs = []
    for i in range(T // SB_BLOCK):
        t0, t1 = i * SB_BLOCK, (i + 1) * SB_BLOCK
        z = jnp.einsum('bhtd,bhsd->bhts', q[:, :, t0:t1], k[:, :, :t1]).astype(jnp.float32) * scale
        t_pos = t0 + jnp.arange(SB_BLOCK)[:, None]
        s_pos = jnp.arange(t1)[None, :]
        mask = s_pos < t_pos
        log_not = jnp.where(mask, jax.nn.log_sigmoid(-z), 0.0)
        log_A = jax.nn.log_sigmoid(z) + lax.cumsum(log_not, axis=3, reverse=True) - log_not
        A = jnp.where(mask, jnp.exp(log_A), 0.0).astype(v.dtype)
        outs.append(jnp.einsum('bhts,bhsd->bhtd', A, v[:, :, :t1]))
    return jnp.concatenate(outs, axis=2)

def sb_layer_mixer(x, mem, k_sb, v_sb, w_in, w_mem_kv, w_out):
    q, qm = jnp.split(x @ w_in, [SB_W], axis=-1)
    o = from_heads(stick_breaking(to_heads(q, SB_HEADS, SB_DIM), k_sb, v_sb))
    m = memory_attention(qm, mem, w_mem_kv)
    return jnp.concatenate([o, m], axis=-1) @ w_out

def peer(x, w_q, subkeys, u_tab, v_tab):
    B, T, D = x.shape
    N = B * T
    xf = x.reshape(N, D)
    q = (xf @ w_q).reshape(N, PEER_HEADS, 2, PEER_QHALF)
    s = jnp.einsum('nhpd,hpkd->nhpk', q, subkeys).astype(jnp.float32)
    top_s, top_i = lax.top_k(s, PEER_TOPK)
    cand_s = (top_s[:, :, 0, :, None] + top_s[:, :, 1, None, :]).reshape(N, PEER_HEADS, PEER_TOPK * PEER_TOPK)
    cand_i = (top_i[:, :, 0, :, None] * PEER_KEYS + top_i[:, :, 1, None, :]).reshape(N, PEER_HEADS, PEER_TOPK * PEER_TOPK)
    best_s, best_pos = lax.top_k(cand_s, PEER_TOPK)
    idx = jnp.take_along_axis(cand_i, best_pos, axis=-1)
    g = jax.nn.softmax(best_s, axis=-1).astype(x.dtype)
    nb = N // PEER_TOKEN_BLOCK
    xb = xf.reshape(nb, PEER_TOKEN_BLOCK, D)
    ib = idx.reshape(nb, PEER_TOKEN_BLOCK, PEER_HEADS, PEER_TOPK)
    gb = g.reshape(nb, PEER_TOKEN_BLOCK, PEER_HEADS, PEER_TOPK)

    def apply_experts(args):
        xt, it, gt = args
        act = jax.nn.gelu(jnp.einsum('nd,nhkd->nhk', xt, u_tab[it]), approximate=False)
        return jnp.einsum('nhk,nhkd->nd', gt * act, v_tab[it])

    return lax.map(apply_experts, (xb, ib, gb)).reshape(B, T, D)

def first_inputs(seed: int = 0) -> dict:
    key = jax.random.key(seed)
    ks = jax.random.split(key, 20)
    nrm = lambda k, shape, scale: jax.random.normal(k, shape, jnp.float32) * scale
    ds = D_MODEL ** -0.5
    beta = DEEPNORM_BETA
    a_col_scale = jnp.concatenate([
        jnp.ones((2 * GLA_K,), jnp.float32),
        jnp.full((GLA_V,), beta, jnp.float32),
        jnp.ones((GLA_V + GLA_GATE_RANK + MEM_W,), jnp.float32)])
    mem_col_scale = jnp.concatenate([jnp.ones((MEM_W,), jnp.float32), jnp.full((MEM_W,), beta, jnp.float32)])
    sb_col_scale = jnp.concatenate([jnp.ones((SB_W,), jnp.float32), jnp.full((SB_W,), beta, jnp.float32)])
    return {
        "x": nrm(ks[0], (BATCH, SEQ, D_MODEL), 1.0),
        "mem": nrm(ks[1], (BATCH, N_MEM, D_MODEL), 1.0),
        "a_w_in": nrm(ks[2], (N_A_LAYERS, D_MODEL, A_IN_W), ds) * a_col_scale,
        "a_w_gate2": nrm(ks[3], (N_A_LAYERS, GLA_GATE_RANK, GLA_K), GLA_GATE_RANK ** -0.5),
        "a_b_gate": nrm(ks[4], (N_A_LAYERS, GLA_K), 0.1),
        "a_head_g": 1.0 + nrm(ks[5], (N_A_LAYERS, GLA_HEADS, GLA_DV), 0.05),
        "a_w_mem_kv": nrm(ks[6], (N_A_LAYERS, D_MODEL, 2 * MEM_W), ds) * mem_col_scale,
        "a_w_out": nrm(ks[7], (N_A_LAYERS, GLA_V + MEM_W, D_MODEL), (GLA_V + MEM_W) ** -0.5 * beta),
        "b_w_in": nrm(ks[8], (N_B_LAYERS, D_MODEL, B_IN_W), ds),
        "b_w_mem_kv": nrm(ks[9], (N_B_LAYERS, D_MODEL, 2 * MEM_W), ds) * mem_col_scale,
        "b_w_out": nrm(ks[10], (N_B_LAYERS, SB_W + MEM_W, D_MODEL), (SB_W + MEM_W) ** -0.5 * beta),
        "sb_w_kv": nrm(ks[11], (D_MODEL, 2 * SB_W), ds) * sb_col_scale,
        "peer_w_q": nrm(ks[12], (DEPTH, D_MODEL, PEER_HEADS * 2 * PEER_QHALF), ds),
        "peer_subkeys": nrm(ks[13], (DEPTH, PEER_HEADS, 2, PEER_KEYS, PEER_QHALF), PEER_QHALF ** -0.5),
        "peer_u": nrm(ks[14], (DEPTH, PEER_EXPERTS, D_MODEL), ds),
        "peer_v": nrm(ks[15], (DEPTH, PEER_EXPERTS, D_MODEL), beta * PEER_HEADS ** -0.5),
        "ln_g": 1.0 + nrm(ks[16], (DEPTH, 2, D_MODEL), 0.05),
        "ln_b": nrm(ks[17], (DEPTH, 2, D_MODEL), 0.02),
    }

def first_block(x, mem, a_w_in, a_w_gate2, a_b_gate, a_head_g, a_w_mem_kv, a_w_out,
              b_w_in, b_w_mem_kv, b_w_out, sb_w_kv, peer_w_q, peer_subkeys, peer_u, peer_v,
              ln_g, ln_b):
    h = x
    k_sb = None
    v_sb = None
    for layer in range(DEPTH):
        if layer < N_A_LAYERS:
            i = layer
            mix = gla_layer_mixer(h, mem, a_w_in[i], a_w_gate2[i], a_b_gate[i], a_head_g[i],
                                  a_w_mem_kv[i], a_w_out[i])
        else:
            if layer == N_A_LAYERS:
                ksb, vsb = jnp.split(h @ sb_w_kv, [SB_W], axis=-1)
                k_sb = to_heads(ksb, SB_HEADS, SB_DIM)
                v_sb = to_heads(vsb, SB_HEADS, SB_DIM)
            j = layer - N_A_LAYERS
            mix = sb_layer_mixer(h, mem, k_sb, v_sb, b_w_in[j], b_w_mem_kv[j], b_w_out[j])
        h = layer_norm(DEEPNORM_ALPHA * h + mix, ln_g[layer, 0], ln_b[layer, 0])
        ffn = peer(h, peer_w_q[layer], peer_subkeys[layer], peer_u[layer], peer_v[layer])
        h = layer_norm(DEEPNORM_ALPHA * h + ffn, ln_g[layer, 1], ln_b[layer, 1])
    return h


GRID_W = 64
HEAD_DIM = D_MODEL // 16
Q_BLOCK = 128
RMS_EPS = 1e-6
NEG_INF = -1e30

NA_HEADS = 4
NA_WIN_H = 8
NA_WIN_W = 16
DIFF_HEADS = 4
DIFF_QK_DIM = HEAD_DIM // 2
DIFF_V_DIM = HEAD_DIM
GQA_Q_HEADS = 4
GQA_KV_HEADS = 2
AXIAL_THETA = 10000.0
DIL_HEADS = 4
DIL_PAIRS = ((128, 1), (512, 4), (2048, 16))
ROPE_THETA = 500000.0
ROPE_FRACTION = 4
D_FF = ((8 * D_MODEL // 3 + 255) // 256) * 256

NA_W = NA_HEADS * HEAD_DIM
DIFF_QK_W = DIFF_HEADS * 2 * DIFF_QK_DIM
DIFF_V_W = DIFF_HEADS * DIFF_V_DIM
GQA_Q_W = GQA_Q_HEADS * HEAD_DIM
GQA_KV_W = GQA_KV_HEADS * HEAD_DIM
DIL_W = DIL_HEADS * HEAD_DIM
IN_SIZES = (NA_W, NA_W, NA_W, DIFF_QK_W, DIFF_QK_W, DIFF_V_W, GQA_Q_W, GQA_KV_W, GQA_KV_W, DIL_W, DIL_W, DIL_W)
IN_WIDTH = sum(IN_SIZES)
MIX_WIDTH = NA_W + DIFF_V_W + GQA_Q_W + DIL_W


def rms_norm(x, gain):
    xf = x.astype(jnp.float32)
    y = xf * lax.rsqrt(jnp.mean(xf * xf, axis=-1, keepdims=True) + RMS_EPS)
    return (y * gain.astype(jnp.float32)).astype(x.dtype)

def rope_tables(pos, dim, theta):
    inv_freq = 1.0 / (theta ** (jnp.arange(0, dim, 2, dtype=jnp.float32) / dim))
    ang = pos.astype(jnp.float32)[:, None] * inv_freq[None, :]
    return jnp.cos(ang), jnp.sin(ang)

def apply_rope(x, cos, sin):
    x1, x2 = jnp.split(x.astype(jnp.float32), 2, axis=-1)
    c = cos[None, :, None, :]
    s = sin[None, :, None, :]
    return jnp.concatenate([x1 * c - x2 * s, x1 * s + x2 * c], axis=-1).astype(x.dtype)

def partial_rope(x, cos, sin, n_rot):
    return jnp.concatenate([apply_rope(x[..., :n_rot], cos, sin), x[..., n_rot:]], axis=-1)

def swiglu(h, w_gate, w_up, w_down):
    return (jax.nn.silu(h @ w_gate) * (h @ w_up)) @ w_down

def split_in_proj(h):
    points = np.cumsum(IN_SIZES)[:-1].tolist()
    return jnp.split(h, points, axis=-1)

def neighborhood_attention(q, k, v, q_gain, k_gain, rel_bias, rows):
    B, S, _ = q.shape
    H, d = NA_HEADS, HEAD_DIM
    q = rms_norm(q.reshape(B, S, H, d), q_gain)
    k = rms_norm(k.reshape(B, S, H, d), k_gain)
    v = v.reshape(B, S, H, d)
    to_grid = lambda t: t.reshape(B, rows, GRID_W, H, d).transpose(0, 3, 1, 2, 4)
    qg, kg, vg = to_grid(q), to_grid(k), to_grid(v)
    kh = min(NA_WIN_H, rows)
    cols = jnp.arange(GRID_W)
    col_idx = jnp.clip(cols - NA_WIN_W // 2, 0, GRID_W - NA_WIN_W)[:, None] + jnp.arange(NA_WIN_W)[None, :]
    col_off = col_idx - cols[:, None] + (NA_WIN_W - 1)
    scale = d ** -0.5

    def row_fn(r):
        rs = jnp.clip(r - kh // 2, 0, rows - kh)
        q_r = lax.dynamic_index_in_dim(qg, r, axis=2, keepdims=False)
        k_rows = lax.dynamic_slice_in_dim(kg, rs, kh, axis=2)
        v_rows = lax.dynamic_slice_in_dim(vg, rs, kh, axis=2)
        k_win = k_rows[:, :, :, col_idx]
        v_win = v_rows[:, :, :, col_idx]
        row_off = rs + jnp.arange(kh) - r + (NA_WIN_H - 1)
        bias = rel_bias[:, row_off][:, :, col_off].transpose(0, 2, 1, 3)
        s = jnp.einsum('bhcd,bhacjd->bhcaj', q_r, k_win).astype(jnp.float32) * scale
        s = s + bias[None].astype(jnp.float32)
        p = jax.nn.softmax(s.reshape(B, H, GRID_W, kh * NA_WIN_W), axis=-1).reshape(s.shape)
        return jnp.einsum('bhcaj,bhacjd->bhcd', p.astype(v.dtype), v_win)

    out = lax.map(row_fn, jnp.arange(rows))
    return out.transpose(1, 0, 3, 2, 4).reshape(B, S, H * d)

def diff_attention(q, k, v, q_gain, k_gain, lq1, lk1, lq2, lk2, out_gain, lambda_init, cos, sin):
    B, S, _ = q.shape
    H, d = DIFF_HEADS, DIFF_QK_DIM
    n_rot = d // ROPE_FRACTION

    def prep(t, g):
        t = partial_rope(rms_norm(t.reshape(B, S, 2 * H, d), g), cos, sin, n_rot)
        return t.reshape(B, S, H, 2, d).transpose(3, 0, 2, 1, 4)

    q12 = prep(q, q_gain)
    k12 = prep(k, k_gain)
    vt = v.reshape(B, S, H, DIFF_V_DIM).transpose(0, 2, 1, 3)
    lam = (jnp.exp(jnp.sum(lq1.astype(jnp.float32) * lk1.astype(jnp.float32)))
           - jnp.exp(jnp.sum(lq2.astype(jnp.float32) * lk2.astype(jnp.float32))) + lambda_init)
    scale = d ** -0.5
    nb = S // Q_BLOCK
    qb = q12.reshape(2, B, H, nb, Q_BLOCK, d).transpose(3, 0, 1, 2, 4, 5)

    def block_fn(qblk):
        s = jnp.einsum('ibhqd,ibhkd->ibhqk', qblk, k12).astype(jnp.float32) * scale
        p = jax.nn.softmax(s, axis=-1)
        a = p[0] - lam * p[1]
        return jnp.einsum('bhqk,bhkd->bhqd', a.astype(vt.dtype), vt)

    o = lax.map(block_fn, qb)
    o = o.transpose(1, 2, 0, 3, 4).reshape(B, H, S, DIFF_V_DIM)
    o = rms_norm(o, out_gain) * (1.0 - lambda_init)
    return o.transpose(0, 2, 1, 3).reshape(B, S, H * DIFF_V_DIM)

def gqa_axial_attention(q, k, v, q_gain, k_gain, row_cs, col_cs):
    B, S, _ = q.shape
    Hq, Hkv, d = GQA_Q_HEADS, GQA_KV_HEADS, HEAD_DIM
    G = Hq // Hkv
    half = d // 2

    def axial(t):
        return jnp.concatenate([apply_rope(t[..., :half], *row_cs), apply_rope(t[..., half:], *col_cs)], axis=-1)

    q = axial(rms_norm(q.reshape(B, S, Hq, d), q_gain))
    k = axial(rms_norm(k.reshape(B, S, Hkv, d), k_gain))
    kt = k.transpose(0, 2, 1, 3)
    vt = v.reshape(B, S, Hkv, d).transpose(0, 2, 1, 3)
    nb = S // Q_BLOCK
    qb = q.reshape(B, nb, Q_BLOCK, Hkv, G, d).transpose(1, 0, 3, 4, 2, 5)
    scale = d ** -0.5

    def block_fn(qblk):
        s = jnp.einsum('bngqd,bnkd->bngqk', qblk, kt).astype(jnp.float32) * scale
        p = jax.nn.softmax(s, axis=-1)
        return jnp.einsum('bngqk,bnkd->bngqd', p.astype(vt.dtype), vt)

    o = lax.map(block_fn, qb)
    return o.transpose(1, 0, 4, 2, 3, 5).reshape(B, S, Hq * d)

def dilated_attention(q, k, v, q_gain, k_gain, cos, sin):
    B, S, _ = q.shape
    H, d = DIL_HEADS, HEAD_DIM
    n_rot = d // ROPE_FRACTION
    q = partial_rope(rms_norm(q.reshape(B, S, H, d), q_gain), cos, sin, n_rot).transpose(0, 2, 1, 3)
    k = partial_rope(rms_norm(k.reshape(B, S, H, d), k_gain), cos, sin, n_rot).transpose(0, 2, 1, 3)
    v = v.reshape(B, S, H, d).transpose(0, 2, 1, 3)
    nb = S // Q_BLOCK
    scale = d ** -0.5

    def block_fn(b):
        t = b * Q_BLOCK + jnp.arange(Q_BLOCK)
        q_b = lax.dynamic_slice_in_dim(q, b * Q_BLOCK, Q_BLOCK, axis=2)
        outs, lses = [], []
        for window, dil in DIL_PAIRS:
            n_side = (window // 2) // dil
            idx = t[:, None] + dil * jnp.arange(-n_side, n_side + 1)[None, :]
            valid = (idx >= 0) & (idx < S)
            idx = jnp.clip(idx, 0, S - 1)
            k_g = jnp.take(k, idx, axis=2)
            v_g = jnp.take(v, idx, axis=2)
            s = jnp.einsum('bhqd,bhqnd->bhqn', q_b, k_g).astype(jnp.float32) * scale
            s = jnp.where(valid[None, None], s, NEG_INF)
            lse = jax.nn.logsumexp(s, axis=-1, keepdims=True)
            p = jnp.exp(s - lse)
            outs.append(jnp.einsum('bhqn,bhqnd->bhqd', p.astype(v.dtype), v_g).astype(jnp.float32))
            lses.append(lse)
        w = jax.nn.softmax(jnp.stack(lses, axis=0), axis=0)
        return jnp.sum(w * jnp.stack(outs, axis=0), axis=0).astype(v.dtype)

    o = lax.map(block_fn, jnp.arange(nb))
    return o.transpose(1, 0, 3, 2, 4).reshape(B, S, H * d)

def second_inputs(seed: int = 0) -> dict:
    key = jax.random.key(seed)
    ks = jax.random.split(key, 32)
    L, D, F = DEPTH, D_MODEL, D_FF

    def w(i, shape, fan_in):
        return jax.random.normal(ks[i], shape, jnp.float32) * (fan_in ** -0.5)

    def gain(i, shape):
        return 1.0 + 0.02 * jax.random.normal(ks[i], shape, jnp.float32)

    def small(i, shape, sd):
        return sd * jax.random.normal(ks[i], shape, jnp.float32)

    return {
        'x': jax.random.normal(ks[0], (BATCH, SEQ, D), jnp.float32),
        'ffn1_norm': gain(1, (L, D)),
        'ffn1_w_gate': w(2, (L, D, F), D),
        'ffn1_w_up': w(3, (L, D, F), D),
        'ffn1_w_down': w(4, (L, F, D), F),
        'mix_norm': gain(5, (L, D)),
        'w_in': w(6, (L, D, IN_WIDTH), D),
        'w_out': w(7, (L, MIX_WIDTH, D), MIX_WIDTH),
        'na_q_norm': gain(8, (L, HEAD_DIM)),
        'na_k_norm': gain(9, (L, HEAD_DIM)),
        'na_rel_bias': small(10, (L, NA_HEADS, 2 * NA_WIN_H - 1, 2 * NA_WIN_W - 1), 0.02),
        'diff_q_norm': gain(11, (L, DIFF_QK_DIM)),
        'diff_k_norm': gain(12, (L, DIFF_QK_DIM)),
        'diff_lambda_q1': small(13, (L, DIFF_QK_DIM), 0.1),
        'diff_lambda_k1': small(14, (L, DIFF_QK_DIM), 0.1),
        'diff_lambda_q2': small(15, (L, DIFF_QK_DIM), 0.1),
        'diff_lambda_k2': small(16, (L, DIFF_QK_DIM), 0.1),
        'diff_out_norm': gain(17, (L, DIFF_V_DIM)),
        'gqa_q_norm': gain(18, (L, HEAD_DIM)),
        'gqa_k_norm': gain(19, (L, HEAD_DIM)),
        'dil_q_norm': gain(20, (L, HEAD_DIM)),
        'dil_k_norm': gain(21, (L, HEAD_DIM)),
        'ffn2_norm': gain(22, (L, D)),
        'ffn2_w_gate': w(23, (L, D, F), D),
        'ffn2_w_up': w(24, (L, D, F), D),
        'ffn2_w_down': w(25, (L, F, D), F),
    }

def second_block(x, ffn1_norm, ffn1_w_gate, ffn1_w_up, ffn1_w_down, mix_norm, w_in, w_out,
              na_q_norm, na_k_norm, na_rel_bias, diff_q_norm, diff_k_norm,
              diff_lambda_q1, diff_lambda_k1, diff_lambda_q2, diff_lambda_k2, diff_out_norm,
              gqa_q_norm, gqa_k_norm, dil_q_norm, dil_k_norm,
              ffn2_norm, ffn2_w_gate, ffn2_w_up, ffn2_w_down):
    B, S, _ = x.shape
    rows = S // GRID_W
    pos = jnp.arange(S, dtype=jnp.int32)
    diff_cs = rope_tables(pos, DIFF_QK_DIM // ROPE_FRACTION, ROPE_THETA)
    dil_cs = rope_tables(pos, HEAD_DIM // ROPE_FRACTION, ROPE_THETA)
    row_cs = rope_tables(pos // GRID_W, HEAD_DIM // 2, AXIAL_THETA)
    col_cs = rope_tables(pos % GRID_W, HEAD_DIM // 2, AXIAL_THETA)

    for l in range(DEPTH):
        h = rms_norm(x, ffn1_norm[l])
        x = x + 0.5 * swiglu(h, ffn1_w_gate[l], ffn1_w_up[l], ffn1_w_down[l])

        h = rms_norm(x, mix_norm[l])
        (na_q, na_k, na_v, df_q, df_k, df_v,
         gq_q, gq_k, gq_v, dl_q, dl_k, dl_v) = split_in_proj(h @ w_in[l])
        o_a = neighborhood_attention(na_q, na_k, na_v, na_q_norm[l], na_k_norm[l], na_rel_bias[l], rows)
        lambda_init = 0.8 - 0.6 * math.exp(-0.3 * l)
        o_b = diff_attention(df_q, df_k, df_v, diff_q_norm[l], diff_k_norm[l],
                             diff_lambda_q1[l], diff_lambda_k1[l], diff_lambda_q2[l], diff_lambda_k2[l],
                             diff_out_norm[l], lambda_init, *diff_cs)
        o_c = gqa_axial_attention(gq_q, gq_k, gq_v, gqa_q_norm[l], gqa_k_norm[l], row_cs, col_cs)
        o_d = dilated_attention(dl_q, dl_k, dl_v, dil_q_norm[l], dil_k_norm[l], *dil_cs)
        o = jnp.concatenate([o_a, o_b, o_c, o_d], axis=-1)
        x = x + o @ w_out[l]

        h = rms_norm(x, ffn2_norm[l])
        x = x + 0.5 * swiglu(h, ffn2_w_gate[l], ffn2_w_up[l], ffn2_w_down[l])
    return x


def setup_inputs(seed=0):
    out = dict(first_inputs(seed))
    for name, value in second_inputs(seed + 1).items():
        if name != "x":
            out[name + "_2"] = value
    return out


def reference(
    x, mem, a_w_in, a_w_gate2, a_b_gate, a_head_g, a_w_mem_kv, a_w_out, b_w_in, b_w_mem_kv,
    b_w_out, sb_w_kv, peer_w_q, peer_subkeys, peer_u, peer_v, ln_g, ln_b, ffn1_norm_2,
    ffn1_w_gate_2, ffn1_w_up_2, ffn1_w_down_2, mix_norm_2, w_in_2, w_out_2, na_q_norm_2,
    na_k_norm_2, na_rel_bias_2, diff_q_norm_2, diff_k_norm_2, diff_lambda_q1_2,
    diff_lambda_k1_2, diff_lambda_q2_2, diff_lambda_k2_2, diff_out_norm_2, gqa_q_norm_2,
    gqa_k_norm_2, dil_q_norm_2, dil_k_norm_2, ffn2_norm_2, ffn2_w_gate_2, ffn2_w_up_2,
    ffn2_w_down_2,
):
    x = first_block(
        x, mem, a_w_in, a_w_gate2, a_b_gate, a_head_g, a_w_mem_kv, a_w_out, b_w_in, b_w_mem_kv,
        b_w_out, sb_w_kv, peer_w_q, peer_subkeys, peer_u, peer_v, ln_g, ln_b,
    )
    return second_block(
        x, ffn1_norm_2, ffn1_w_gate_2, ffn1_w_up_2, ffn1_w_down_2, mix_norm_2, w_in_2, w_out_2,
        na_q_norm_2, na_k_norm_2, na_rel_bias_2, diff_q_norm_2, diff_k_norm_2, diff_lambda_q1_2,
        diff_lambda_k1_2, diff_lambda_q2_2, diff_lambda_k2_2, diff_out_norm_2, gqa_q_norm_2,
        gqa_k_norm_2, dil_q_norm_2, dil_k_norm_2, ffn2_norm_2, ffn2_w_gate_2, ffn2_w_up_2,
        ffn2_w_down_2,
    )


_drawn_inputs = setup_inputs


def setup_inputs(seed=0):
    import zlib

    import numpy as np

    out = dict(_drawn_inputs(seed))
    spreads = {}
    factors = {'a_b_gate': 3.737,
     'a_head_g': 3.386,
     'ffn1_norm_2': 4.452,
     'mix_norm_2': 3.334,
     'na_q_norm_2': 8.0,
     'na_k_norm_2': 8.0,
     'na_rel_bias_2': 36.416,
     'diff_q_norm_2': 6.44,
     'diff_k_norm_2': 6.405,
     'diff_lambda_q2_2': 2.794,
     'diff_lambda_k2_2': 4.448,
     'diff_out_norm_2': 5.266,
     'gqa_q_norm_2': 8.0,
     'gqa_k_norm_2': 8.0,
     'dil_q_norm_2': 8.0,
     'dil_k_norm_2': 8.0,
     'ffn2_norm_2': 5.472,
     'diff_lambda_k1_2': 3.292}
    for name, (base, spread) in spreads.items():
        noise = np.random.default_rng([zlib.crc32(name.encode()), seed]).standard_normal(out[name].shape)
        drawn = base * np.exp(spread * noise) if base else spread * noise
        out[name] = __import__('jax').numpy.asarray(drawn.astype(out[name].dtype))
    for name, factor in factors.items():
        out[name] = (out[name] * factor).astype(out[name].dtype)
    return out
```

```python
import math
from contextlib import ExitStack

import concourse.bass as bass
from concourse import mybir

P = 128
ALU = mybir.AluOpType
ACT = mybir.ActivationFunctionType
F32 = mybir.dt.float32
FR = mybir.dt.float32r
U32 = mybir.dt.uint32
AX = mybir.AxisListType.X

DEPTH = 2
ALPHA = (2.0 * DEPTH) ** 0.25
NEG = -1.0e30
LOWEST = -3.0e38
NRAW = 5
NHALF = 4
PARTS = 2
GP = P // PARTS

ENGINES = ("pe", "act", "dve", "pool", "sp")


class Done:

    def __init__(self, eng):
        self.eng, self.used, self.val, self.sem = eng, False, 0, None


class Landed:

    def __init__(self, sem, val):
        self.sem, self.val, self.used = sem, val, True


class Queues:

    def __init__(self):
        self.q = {e: [] for e in ENGINES}
        self.fence = {e: [] for e in ENGINES}
        self.last = {}

    def op(self, eng, fn, after=()):
        need = [a for a in after if a is not None] + self.fence[eng]
        self.fence[eng] = []
        for a in need:
            a.used = True
        t = Done(eng)
        self.q[eng].append((fn, need, t, None))
        self.last[eng] = t
        return t

    def dma(self, eng, fn, landed, after=()):
        need = [a for a in after if a is not None] + self.fence[eng]
        self.fence[eng] = []
        for a in need:
            a.used = True
        self.q[eng].append((fn, need, None, landed))
        return landed

    def phase(self, engines=("pe", "act", "dve", "pool")):
        now = [self.last[e] for e in ("pe", "act", "dve", "pool") if e in self.last]
        for e in engines:
            self.fence[e] = list(now)

    def count(self, sems):
        for e in ENGINES:
            n = 0
            for _, _, t, landed in self.q[e]:
                if t is not None and t.used:
                    n += 1
                    t.val, t.sem = n, sems[e]

    def emit(self, e, engine, sems):
        seen = {}
        for fn, need, t, landed in self.q[e]:
            want = {}
            for a in need:
                want[a.sem] = max(want.get(a.sem, 0), a.val)
            for s, v in want.items():
                if seen.get(s, 0) < v:
                    engine.wait_ge(s, v)
                    seen[s] = v
            ins = fn(engine)
            if landed is not None:
                ins.then_inc(landed.sem, 16)
            elif t.used:
                ins.then_inc(sems[e], 1)


class Bank:
    def __init__(self, ap):
        self.ap, self.free = ap, []


class Arena:
    def __init__(self, big, lo=0, hi=32768):
        self.big, self.at, self.hi = big, lo, hi

    def __call__(self, cols):
        a = self.big[:, self.at:self.at + cols]
        self.at += cols
        assert self.at <= self.hi, self.at
        return a


class Program:
    def __init__(self, nc, ctx, n_units, small, out, upto):
        self.nc, self.ctx, self.Q = nc, ctx, Queues()
        self.small, self.out, self.upto = small, out, upto
        self.n_units = n_units
        self.order = []

        def sb(name, shape, dt):
            return ctx.enter_context(nc.sbuf_tensor(name, shape, dt))

        def sem(name):
            return ctx.enter_context(nc.semaphore(name))

        self.sem = sem
        self.sems = {e: sem("s_" + e) for e in ENGINES}
        self.BIG = sb("BIG", [P, 32768], F32)
        self.H = sb("H", [P, 2, 1024], F32)
        self.XTh = sb("XTh", [P, 8, 256], FR)
        self.XTl = sb("XTl", [P, 8, 256], FR)
        self.RAW = sb("RAW", [P, NRAW, 1024], F32)
        self.WH = sb("WH", [P, NHALF, 512], FR)
        self.WL = sb("WL", [P, NHALF, 512], FR)
        self.OHA = sb("OHA", [P, 8, 128], F32)
        self.OHB = sb("OHB", [P, 8, GP], F32)
        self.ABG = sb("ABG", [P, 3, 256], F32)
        self.GH = sb("GH", [P, 2, 256], FR)
        self.GL = sb("GL", [P, 2, 256], FR)
        self.CST = sb("CST", [P, 256 + 8 + 48], F32)
        self.IDENT = self.CST[:, 0:128]
        self.IOTA = self.CST[:, 128:256]
        self.EPS5 = self.CST[:, 256:257]
        self.EPS6 = self.CST[:, 257:258]
        self.ONE = self.CST[:, 258:259]
        self.COLS = self.CST[:, 264:312]
        self.B = [Bank(ctx.enter_context(nc.psum_tensor(f"ps{i}", [P, 512], F32))) for i in range(8)]
        self.raw_sem = [sem(f"s_raw{i}") for i in range(NRAW)]
        self.raw_free = [[] for _ in range(n_units)]
        self.half_tok = {}
        self.half_done = {}
        self.n_split = self.n_taken = 0
        self.loads = 0
        self.share = 4

    def mm(self, out, lhsT, rhs, start, stop, after=(), loose=False):
        return self.Q.op("pe", lambda e: e.matmul(out, lhsT, rhs, start=start, stop=stop, skip_group_check=loose), after)

    def tr(self, out, in_, after=()):
        n = in_.shape[0]
        ident = self.IDENT[0:n, 0:n]
        return self.Q.op("pe", lambda e: e.transpose(out, in_, ident), after)

    def act(self, out, in_, func, after=(), scale=1.0, bias=None, accum=None):
        def go(e):
            kw = {}
            if bias is not None:
                kw["bias"] = bias
            if accum is not None:
                kw["accum_out"] = accum
            return e.activation(out, in_, func, scale=scale, **kw)
        return self.Q.op("act", go, after)

    def tt(self, out, a, b, op, after=(), eng="dve"):
        return self.Q.op(eng, lambda e: e.tensor_tensor(out, a, b, op), after)

    def ts(self, out, a, s1, s2, op0, op1=None, after=(), eng="dve"):
        if op1 is None:
            return self.Q.op(eng, lambda e: e.tensor_scalar(out, a, s1, None, op0), after)
        return self.Q.op(eng, lambda e: e.tensor_scalar(out, a, s1, s2, op0, op1), after)

    def stt(self, out, a, s, b, op0, op1, after=()):
        return self.Q.op("dve", lambda e: e.scalar_tensor_tensor(out=out, in0=a, scalar=s, in1=b, op0=op0, op1=op1), after)

    def cp(self, out, in_, after=(), eng="dve"):
        if eng == "act":
            return self.act(out, in_, ACT.Copy, after)
        return self.Q.op(eng, lambda e: e.tensor_copy(out, in_), after)

    def red(self, out, in_, op, after=(), negate=None):
        return self.Q.op("dve", lambda e: e.tensor_reduce(out, in_, AX, op, negate=negate), after)

    def rcp(self, out, in_, after=()):
        return self.Q.op("dve", lambda e: e.reciprocal(out, in_), after)

    def memset(self, out, v, after=(), eng="pool"):
        return self.Q.op(eng, lambda e: e.memset(out, v), after)

    def load(self, dst, src, after=()):
        self.loads += 1
        landed = Landed(self.sem(f"s_ld{self.loads}"), 16)
        return self.Q.dma("act", lambda e: e.dma_start(dst, src), landed, after)

    def landed(self, u):
        return Landed(self.raw_sem[u % NRAW], 16 * (u // NRAW + 1))

    def split_next(self):
        j = self.n_split
        if j >= 2 * self.n_units:
            return
        self.n_split += 1
        u, s = j // 2, j % NHALF
        raw = self.RAW[:, u % NRAW, (j % 2) * 512:(j % 2) * 512 + 512]
        came, old = self.landed(u), self.half_done.get(j - NHALF)
        hi = self.act(self.WH[:, s, :], raw, ACT.Copy, [came, old])
        eng = "pool" if j % self.share == self.share - 1 else "dve"
        lo = self.tt(self.WL[:, s, :], raw, self.WH[:, s, :].bitcast(F32), ALU.subtract, [came, hi, old], eng)
        self.half_tok[j] = lo
        self.raw_free[u] += [hi, lo]

    def take(self, key=None):
        j = self.n_taken
        if j % 2 == 0:
            self.order.append(key)
        self.n_taken += 1
        while self.n_split <= j:
            self.split_next()
        s = j % NHALF
        return j, self.WH[:, s, :], self.WL[:, s, :], self.half_tok[j]

    def release(self, j, tok):
        self.half_done[j] = tok
        while self.n_split <= j + NHALF and self.n_split < 2 * self.n_units:
            self.split_next()

    def stream_dmas(self, w):
        for u in range(self.n_units):
            after = self.raw_free[u - NRAW] if u >= NRAW else []
            dst = self.RAW[:, u % NRAW, :]
            src = w[u]
            self.Q.dma("sp", self.starter(dst, src), self.landed(u), after)

    def starter(self, dst, src):
        return lambda e: e.dma_start(dst, src)

    def three(self, out, ah, al, bh, bl, start, stop, after):
        self.mm(out, ah, bh, start, False, after)
        self.mm(out, ah, bl, False, False)
        return self.mm(out, al, bh, False, stop)

    def cols_unit(self, key, out, after):
        for half in range(2):
            j, wh, wl, ready = self.take((key))
            for c in range(4):
                cc = half * 4 + c
                w = slice(c * 128, c * 128 + 128)
                t = self.three2(out, wh[:, w], wl[:, w], self.XTh[:, cc, :], self.XTl[:, cc, :], cc == 0, cc == 7,
                                [ready, *after])
                after = []
            self.release(j, t)
        return t

    def three2(self, out, wh, wl, xh, xl, start, stop, after):
        self.mm(out, wh, xh, start, False, after)
        self.mm(out, wh, xl, False, False)
        return self.mm(out, wl, xh, False, stop)

    def rows_block(self, keys, outs, width, after):
        per = 512 // width
        c = 0
        for key in keys:
            for half in range(2):
                j, wh, wl, ready = self.take(key)
                for k in range(per):
                    w = slice(k * width, k * width + width)
                    for blk in range(2):
                        tb = slice(blk * 128, blk * 128 + 128)
                        t = self.three(outs[blk], self.XTh[:, c, tb], self.XTl[:, c, tb], wh[:, w], wl[:, w],
                                       c == 0, c == 7, [ready, *after])
                    after = []
                    c += 1
                self.release(j, t)
        return t

    def depth_unit(self, key, ah, al, first, last, after):
        for half in range(2):
            j, wh, wl, ready = self.take(key)
            for blk in range(2):
                tb = slice(blk * 128, blk * 128 + 128)
                t = self.three(self.B[blk * 2 + half].ap[:, :], ah[:, tb], al[:, tb], wh, wl, first, last, [ready, *after])
            self.release(j, t)
        return t

    def to_xt(self, src, after, gain=None):
        toks = []
        for g in range(4):
            b = self.B[4 + g]
            for k in range(2):
                for blk in range(2):
                    c = 2 * g + k
                    t = self.tr(b.ap[:, k * 256 + blk * 128:k * 256 + blk * 128 + 128], src[:, blk, c * 128:c * 128 + 128],
                                [*after, *b.free])
            hi, lo = self.XTh[:, 2 * g:2 * g + 2, :], self.XTl[:, 2 * g:2 * g + 2, :]
            ps = b.ap[:, :].rearrange("p (a n) -> p a n", a=2)
            if gain is None:
                h = self.cp(hi, ps, [t], "act")
                l = self.tt(lo, ps, hi.bitcast(F32), ALU.subtract, [h, t])
                b.free = [h, l]
                toks += [h, l]
            else:
                b.free = []
                hs = [self.act(self.XTh[:, 2 * g + k, :], ps[:, k, :], ACT.Copy, [t], scale=gain[:, 2 * g + k:2 * g + k + 1])
                      for k in range(2)]
                for k in range(2):
                    c, h = 2 * g + k, hs[1]
                    l = self.stt(self.XTl[:, c, :], ps[:, k, :], gain[:, c:c + 1], self.XTh[:, c, :].bitcast(F32), ALU.mult,
                                 ALU.subtract, [h, t])
                    b.free += [h, l]
                    toks += [h, l]
        return toks

    def split_xt(self, src, after):
        h = self.cp(self.XTh[:, :, :], src, after, "act")
        l = self.tt(self.XTl[:, :, :], src, self.XTh[:, :, :].bitcast(F32), ALU.subtract, [h, *after])
        return [h, l]

    def layer_norm(self, z, gb, sc, after, gb_in):
        toks = []
        for blk in range(2):
            st, mv, sd = sc[:, 20 * blk:20 * blk + 12], sc[:, 20 * blk + 12:20 * blk + 14], sc[:, 20 * blk + 14:20 * blk + 15]
            rs = sc[:, 20 * blk + 15:20 * blk + 16]
            a = [self.bn(st[:, 6 * k:6 * k + 6], z[:, blk, 512 * k:512 * k + 512], after) for k in range(2)]
            m = self.bn_end(mv, st, a)
            s = self.act(sd, mv[:, 1:2], ACT.Sqrt, [m], bias=self.EPS5)
            r = self.rcp(rs, sd, [s])
            y = self.stt(z[:, blk, :], z[:, blk, :], mv[:, 0:1], gb[:, 0, :], ALU.subtract, ALU.mult, [m, gb_in, *a])
            toks.append(self.stt(self.H[:, blk, :], z[:, blk, :], rs, gb[:, 1, :], ALU.mult, ALU.add, [y, r, gb_in]))
        return toks

    def bn(self, out, in_, after):
        return self.Q.op("dve", lambda e: e.bn_stats(out, in_), after)

    def bn_end(self, out, in_, after):
        return self.Q.op("dve", lambda e: e.bn_aggr(out, in_), after)

    def rms_rows(self, xn, sc, after):
        toks = []
        for blk in range(2):
            ss, sd, rs = sc[:, 4 * blk:4 * blk + 1], sc[:, 4 * blk + 1:4 * blk + 2], sc[:, 4 * blk + 2:4 * blk + 3]
            a = self.act(xn[:, blk, :], self.H[:, blk, :], ACT.Square, after, accum=ss)
            s = self.act(sd, ss, ACT.Sqrt, [a], scale=1.0 / 1024, bias=self.EPS6)
            r = self.rcp(rs, sd, [s])
            toks.append(self.ts(xn[:, blk, :], self.H[:, blk, :], rs, None, ALU.mult, None, [r, a, *after]))
        return toks

    def attention(self, heads, ar):
        n = len(heads)
        T = ar(2 * 512).rearrange("p (r n) -> p r n", r=2)
        E = ar(2 * 512).rearrange("p (r n) -> p r n", r=2)
        PT = ar(2 * 512).rearrange("p (r n) -> p r n", r=2)
        st = ar(3 * 6).rearrange("p (r n) -> p r n", r=3)
        t_free, e_free, pt_free = [[], []], [[], []], [[], []]
        exps, rcps, pts, ends = {}, {}, {}, {}

        def scores(i):
            h, b = heads[i], self.B[i % 2]
            for blk in range(2):
                t = self.mm(b.ap[:, blk * 256:blk * 256 + 256], h["q"][:, blk * 128:blk * 128 + 128], h["k"], True, True,
                            [*h["after"], *b.free])
            src, ready = b.ap[:, :].rearrange("p (b n) -> p b n", b=2), t
            if h["bias"] is not None:
                dst = T[:, i % 2, :].rearrange("p (b n) -> p b n", b=2)
                ready = self.tt(dst, src, h["bias"], ALU.add, [t, *t_free[i % 2], *h["bias_after"]])
                b.free = [ready]
                src = dst
            s = st[:, i % 3, :]
            old = [ends[i - 3]] if i >= 3 else []
            m = self.red(s[:, 0:2], src, ALU.max, [ready, *old], negate=True)
            ex = []
            for blk in range(2):
                ex.append(self.act(E[:, i % 2, blk * 256:blk * 256 + 256], src[:, blk, :], ACT.Exp,
                                   [m, ready, *e_free[i % 2], *old], bias=s[:, blk:blk + 1], accum=s[:, 2 + blk:3 + blk]))
            if h["bias"] is not None:
                t_free[i % 2] = [m, *ex]
            else:
                b.free = [m, *ex]
            exps[i] = ex
            rcps[i] = self.rcp(s[:, 4:6], s[:, 2:4], [*ex, *old])

        def turn(i):
            b = self.B[2 + i % 2]
            for blk in range(2):
                for sbk in range(2):
                    t = self.tr(b.ap[:, sbk * 256 + blk * 128:sbk * 256 + blk * 128 + 128],
                                E[:, i % 2, blk * 256 + sbk * 128:blk * 256 + sbk * 128 + 128], [exps[i][blk], *b.free])
            e_free[i % 2] = [t]
            c = self.cp(PT[:, i % 2, :], b.ap[:, :], [t, *pt_free[i % 2]], "act" if i % 2 else "dve")
            b.free = [c]
            pts[i] = c

        def values(i):
            h, b = heads[i], self.B[4 + i % 2]
            for blk in range(2):
                for sbk in range(2):
                    t = self.mm(b.ap[:, blk * 64:blk * 64 + 64], PT[:, i % 2, sbk * 256 + blk * 128:sbk * 256 + blk * 128 + 128],
                                h["v"][sbk], sbk == 0, sbk == 1, [pts[i], *b.free, *h["after"]])
            pt_free[i % 2] = [t]
            r = st[:, i % 3, 4:6].unsqueeze(2).to_broadcast([P, 2, 64])
            e = h["finish"](b.ap[:, 0:128].rearrange("p (b d) -> p b d", b=2), r, [t, rcps[i]])
            b.free = [e]
            ends[i] = e

        for i in range(n + 2):
            if i < n:
                scores(i)
            if 1 <= i <= n:
                turn(i - 1)
            if i >= 2:
                values(i - 2)
        return [ends[n - 1], ends[n - 2]]

    def mem_attention(self, layer, ar, qmT, O, after):
        memT = ar(8 * 256).rearrange("p (c n) -> p c n", c=8)
        kmT = ar(2 * 256).rearrange("p (c n) -> p c n", c=2)
        vm = ar(2 * 256).rearrange("p (c n) -> p c n", c=2)
        m_in = self.load(memT, self.small["memT"], [])
        xt = self.split_xt(memT, [m_in, *after])
        ready = []
        for p in range(2):
            b = self.B[6 + p]
            t = self.cols_unit(("km", layer, p), b.ap[:, 0:256], [*xt, *b.free])
            b.free = [self.cp(kmT[:, p, :], b.ap[:, 0:256], [t], "act")]
            ready += b.free
        outs = [self.B[4], self.B[5]]
        t = self.rows_block([("vm", layer, k) for k in range(2)], [b.ap[:, 0:256] for b in outs], 256,
                            [*outs[0].free, *outs[1].free])
        for blk in range(2):
            outs[blk].free = [self.cp(vm[:, blk, :], outs[blk].ap[:, 0:256], [t], "act")]
            ready += outs[blk].free

        def finish(col):
            return lambda ps, r, aft: self.tt(O[:, :, col:col + 64], ps, r, ALU.mult, aft)

        heads = []
        for h in range(4):
            o = (h % 2) * 64
            heads.append(dict(q=qmT[o:o + 64, h // 2, :], k=kmT[o:o + 64, h // 2, :],
                              v=[vm[:, s, h * 64:h * 64 + 64] for s in range(2)], bias=None, after=ready,
                              finish=finish(768 + 64 * h)))
        return self.attention(heads, ar)

    def project_out(self, name, layer, O, after):
        xt = self.to_xt(O, after)
        free = [f for b in self.B[0:4] for f in b.free]
        for c in range(8):
            t = self.depth_unit((name, layer, c), self.XTh[:, c, :], self.XTl[:, c, :], c == 0, c == 7,
                                [*xt, *free] if c == 0 else [])
        return t

    def deepnorm(self, ar, gb, gb_in, t):
        Z = ar(2048).rearrange("p (b n) -> p b n", b=2)
        sc = ar(48)
        zs = []
        for blk in range(2):
            for half in range(2):
                b = self.B[blk * 2 + half]
                cols = slice(512 * half, 512 * half + 512)
                z = self.stt(Z[:, blk, cols], self.H[:, blk, cols], ALPHA, b.ap[:, :], ALU.mult, ALU.add, [t, self.h_in])
                b.free = [z]
                zs.append(z)
        return self.layer_norm(Z, gb, sc, zs, gb_in)

    def load_gb(self, ar, i, after=()):
        gb = ar(2048).rearrange("p (a n) -> p a n", a=2)
        src = self.small["ln"][i].unsqueeze(0).to_broadcast([P, 2, 1024])
        return gb, self.load(gb, src, after)

    def gla_mixer(self, xt):
        Q = self.Q
        ar = Arena(self.BIG)
        O = ar(2048).rearrange("p (b n) -> p b n", b=2)
        gb, gb_in = self.load_gb(ar, 0)
        MASK, TRI = ar(128), ar(128)
        cst_in = self.load(self.BIG[:, ar.at - 256:ar.at], self.small["gla_c"])
        hg = ar(768)
        hg_in = self.load(hg, self.small["head_g"].to_broadcast([P, 768]))
        wg = ar(384)
        wg_in = self.load(wg[0:17, :], self.small["wg2"])
        glrT = ar(256)
        ones = self.memset(glrT[0:32, :], 1.0)
        qT, kT = (ar(768).rearrange("p (c n) -> p c n", c=3) for _ in range(2))
        qmT = ar(512).rearrange("p (c n) -> p c n", c=2)
        vr = ar(3072).rearrange("p (b n) -> p b n", b=2)
        LG = ar(768).rearrange("p (b n) -> p b n", b=2)
        t1 = ar(768).rearrange("p (b n) -> p b n", b=2)
        t2 = ar(768).rearrange("p (b n) -> p b n", b=2)

        b = self.B[4]
        t = self.cols_unit(("glr", 0), b.ap[:, 0:256], [*xt, *b.free])
        g = self.cp(glrT[0:16, :], b.ap[0:16, 0:256], [t, ones])
        b.free = [g]
        zt = []
        for blk in range(2):
            bb = self.B[blk]
            z = self.mm(bb.ap[:, 0:384], glrT[0:17, blk * 128:blk * 128 + 128], wg[0:17, :], True, True, [g, ones, wg_in])
            a = self.act(t1[:, blk, :], bb.ap[:, 0:384], ACT.Abs, [z])
            e = self.act(t2[:, blk, :], t1[:, blk, :], ACT.Exp, [a], scale=-1.0)
            l = self.act(t1[:, blk, :], t2[:, blk, :], ACT.Ln, [e], bias=self.ONE)
            s = self.stt(LG[:, blk, :], bb.ap[:, 0:384], 0.0, t1[:, blk, :], ALU.min, ALU.subtract, [l, z])
            bb.free = [a, s]
            zt.append(s)
        qk = []
        for n, (dst, key, k, sc) in enumerate([(qT, "aq", 0, 0.125), (qT, "aq", 1, 0.125), (qT, "aq", 2, 0.125),
                                               (kT, "ak", 0, 1.0), (kT, "ak", 1, 1.0), (kT, "ak", 2, 1.0),
                                               (qmT, "aqm", 0, 0.125), (qmT, "aqm", 1, 0.125)]):
            b = self.B[4 + n % 4]
            t = self.cols_unit((key, k), b.ap[:, 0:256], b.free)
            b.free = [self.act(dst[:, k, :], b.ap[:, 0:256], ACT.Copy, [t], scale=sc)]
            qk += b.free
        BT, EB, EN, EK = (ar(768).rearrange("p (c n) -> p c n", c=3) for _ in range(4))
        for p in range(3):
            for blk in range(2):
                bb, o = self.B[2 + p // 2], (p % 2) * 256 + blk * 128
                t = self.mm(bb.ap[:, o:o + 128], LG[:, blk, p * 128:p * 128 + 128], TRI, True, True, [*zt, cst_in, *bb.free])
        c0 = self.cp(BT[:, 0:2, :], self.B[2].ap[:, :].rearrange("p (c n) -> p c n", c=2), [t])
        c1 = self.cp(BT[:, 2, :], self.B[3].ap[:, 0:256], [t])
        self.B[2].free, self.B[3].free = [c0], [c1]
        eb = self.act(EB, BT, ACT.Exp, [c0, c1])
        en = self.act(EN, BT, ACT.Exp, [c0, c1], scale=-1.0)
        ek = []
        for p in range(3):
            for n in range(4):
                ek.append(self.act(EK[:, p, 64 * n:64 * n + 64], BT[:, p, 64 * n:64 * n + 64], ACT.Exp, [c0, c1], scale=-1.0,
                                   bias=BT[:, p, 64 * n + 63:64 * n + 64]))
        qd = self.tt(qT, qT, EB, ALU.mult, [*qk, eb])
        ke = self.tt(EK, EK, kT, ALU.mult, [*qk, *ek], "pool")
        ki = self.tt(EN, EN, kT, ALU.mult, [*qk, en])
        vt = []
        for c in range(3):
            outs = [self.B[4 + 2 * (c % 2)], self.B[5 + 2 * (c % 2)]]
            t = self.rows_block([("avr", c, k) for k in range(4)], [x.ap[:, :] for x in outs], 512,
                                [*outs[0].free, *outs[1].free])
            for blk in range(2):
                outs[blk].free = [self.cp(vr[:, blk, c * 512:c * 512 + 512], outs[blk].ap[:, :], [t], "act")]
                vt += outs[blk].free
        KE = ar(768).rearrange("p (b n) -> p b n", b=2)
        kt = []
        for blk in range(2):
            b = self.B[blk]
            for p in range(3):
                t = self.tr(b.ap[:, p * 128:p * 128 + 128], EK[:, p, blk * 128:blk * 128 + 128], [ke, *b.free])
            b.free = [self.cp(KE[:, blk, :], b.ap[:, 0:384], [t])]
            kt += b.free
        AT = ar(3 * 512).rearrange("p (c n) -> p c n", c=3)
        at = []
        for p in range(3):
            b = self.B[2 + p % 2]
            t = None
            for hh in range(2):
                turn = t
                for blk in range(2):
                    o, tb = hh * 64, slice(blk * 128, blk * 128 + 128)
                    t = self.mm(b.ap[:, hh * 256 + blk * 128:hh * 256 + blk * 128 + 128], EN[o:o + 64, p, tb],
                                qT[o:o + 64, p, tb], True, True, [qd, ki, turn, *b.free])
            at.append(self.tt(AT[:, p, :].rearrange("p (a n) -> p a n", a=4), b.ap[:, :].rearrange("p (a n) -> p a n", a=4),
                              MASK.unsqueeze(1).to_broadcast([P, 4, 128]), ALU.mult, [t, cst_in]))
            b.free = [at[-1]]
        S = ar(9 * 128).rearrange("p (c n v) -> p c n v", c=3, n=3)
        sready = []
        for n in range(3):
            for p in range(3):
                b = self.B[4 + (n * 3 + p) % 4]
                cb = slice((n % 2) * 64, (n % 2) * 64 + 64)
                t = self.mm(b.ap[:, 0:256], KE[cb, n // 2, p * 128:p * 128 + 128], vr[cb, n // 2, p * 256:p * 256 + 256],
                            True, True, [*kt, *vt, *b.free])
                b.free = []
                for hh in range(2):
                    o = slice(hh * 64, hh * 64 + 64)
                    du = b.ap[o, hh * 128:hh * 128 + 128]
                    if n == 0:
                        s = self.cp(S[o, p, 0, :], du, [t])
                    else:
                        s = self.stt(S[o, p, n, :], S[o, p, n - 1, :], EB[o, p, 64 * n + 63:64 * n + 64], du, ALU.mult, ALU.add,
                                     [t, eb, *sready])
                    b.free.append(s)
                sready += b.free
        osb = ar(1536).rearrange("p (b n) -> p b n", b=2)
        sq = ar(1536).rearrange("p (b n) -> p b n", b=2)
        ot = []
        for p in range(3):
            b = self.B[p % 2]
            t = None
            for hh in range(2):
                o = slice(hh * 64, hh * 64 + 64)
                turn = t
                for blk in range(2):
                    col = hh * 256 + blk * 128
                    rest = [n for n in (2 * blk, 2 * blk + 1) if n >= 1]
                    t = self.mm(b.ap[:, col:col + 128], AT[:, p, col:col + 128],
                                vr[:, blk, (2 * p + hh) * 128:(2 * p + hh) * 128 + 128], True, False,
                                [at[p], turn, *vt, *b.free, *sready], loose=True)
                    for n in rest:
                        t = self.mm(b.ap[(n % 2) * 64:(n % 2) * 64 + 64, col:col + 128], qT[o, p, n * 64:n * 64 + 64],
                                    S[o, p, n - 1, :], False, n == rest[-1], [], loose=True)
            b.free = []
            for hh in range(2):
                c = self.cp(osb[:, :, (2 * p + hh) * 128:(2 * p + hh) * 128 + 128],
                            b.ap[:, hh * 256:hh * 256 + 256].rearrange("p (b n) -> p b n", b=2), [t], "act")
                b.free.append(c)
            ot += b.free
        s1 = self.tt(sq, osb, osb, ALU.mult, ot)
        sc = ar(48)
        s2 = self.red(sc[:, 0:12], sq.rearrange("p b (h n) -> p (b h) n", h=6), ALU.add, [s1])
        s3 = self.act(sc[:, 12:24], sc[:, 0:12], ACT.Sqrt, [s2], scale=1.0 / 128, bias=self.EPS5)
        s4 = self.rcp(sc[:, 24:36], sc[:, 12:24], [s3])
        s5 = self.tt(sq.rearrange("p b (h n) -> p (b h) n", h=6), osb.rearrange("p b (h n) -> p (b h) n", h=6),
                     sc[:, 24:36].unsqueeze(2).to_broadcast([P, 12, 128]), ALU.mult, [s4, s2])
        s6 = self.tt(sq, sq, hg.unsqueeze(1).to_broadcast([P, 2, 768]), ALU.mult, [s5, hg_in])
        s7 = self.act(vr[:, :, 768:1536], vr[:, :, 768:1536], ACT.Silu, vt)
        s8 = self.tt(O[:, :, 0:768], sq, vr[:, :, 768:1536], ALU.mult, [s6, s7])
        end = self.mem_attention(0, ar, qmT, O, [Q.last["pe"]])
        t = self.project_out("awo", 0, O, [s8, *end])
        return self.deepnorm(ar, gb, gb_in, t)

    def sb_mixer(self, xt):
        Q = self.Q
        ar = Arena(self.BIG)
        O = ar(2048).rearrange("p (b n) -> p b n", b=2)
        gb, gb_in = self.load_gb(ar, 2)
        LOW, ONES, MASK, NMASK = ar(128), ar(128), ar(128), ar(128)
        cst_in = self.load(self.BIG[:, ar.at - 512:ar.at], self.small["sb_c"])
        qT, kT = (ar(6 * 256).rearrange("p (c n) -> p c n", c=6) for _ in range(2))
        qmT = ar(512).rearrange("p (c n) -> p c n", c=2)
        v = ar(1536).rearrange("p (b n) -> p b n", b=2)
        ready = []
        todo = [(kT, "bk", k, 1.0) for k in range(6)] + [(qT, "bq", k, 0.125) for k in range(6)]
        todo += [(qmT, "bqm", k, 0.125) for k in range(2)]
        aft = xt
        for n, (dst, key, k, sc) in enumerate(todo):
            b = self.B[4 + n % 4]
            t = self.cols_unit((key, k), b.ap[:, 0:256], [*aft, *b.free])
            aft = []
            b.free = [self.act(dst[:, k, :], b.ap[:, 0:256], ACT.Copy, [t], scale=sc)]
            ready += b.free
        for c, width in ((0, 512), (1, 256)):
            outs = [self.B[2 * c], self.B[2 * c + 1]]
            t = self.rows_block([("bv", c, k) for k in range(4 if c == 0 else 2)], [x.ap[:, 0:width] for x in outs], width,
                                [*outs[0].free, *outs[1].free])
            for blk in range(2):
                outs[blk].free = [self.cp(v[:, blk, c * 512:c * 512 + width], outs[blk].ap[:, 0:width], [t], "act")]
                ready += outs[blk].free
        A1, A2, SP, AT = (ar(2 * 384).rearrange("p (r n) -> p r n", r=2) for _ in range(4))
        a1_free, a2_free, sp_free, at_free = [[], []], [[], []], [[], []], [[], []]
        mids, ats, ends = {}, {}, {}

        def scores(h):
            b, o, p, r = self.B[h % 2], slice((h % 2) * 64, (h % 2) * 64 + 64), h // 2, h % 2
            self.mm(b.ap[:, 0:256], kT[o, p, 0:128], qT[o, p, 0:256], True, True, [*ready, *b.free], loose=True)
            t = self.mm(b.ap[:, 256:384], kT[o, p, 128:256], qT[o, p, 128:256], False, True, loose=True)
            z = b.ap[:, 0:384]
            a = self.act(A1[:, r, :], z, ACT.Abs, [t, *a1_free[r]])
            e = self.act(A2[:, r, :], A1[:, r, :], ACT.Exp, [a, *a2_free[r]], scale=-1.0)
            l = self.act(A1[:, r, :], A2[:, r, :], ACT.Ln, [e], bias=self.ONE)
            s = self.stt(SP[:, r, :], z, 0.0, A1[:, r, :], ALU.max, ALU.add, [l, t, *sp_free[r]])
            diag = SP[:, r, :].rearrange("p (a n) -> p a n", a=3)[:, 0:3:2, :]
            m = self.tt(diag, diag, MASK.unsqueeze(1).to_broadcast([P, 2, 128]), ALU.mult, [s, cst_in])
            a1_free[r], a2_free[r] = [s], [l]
            mids[h] = [a, s, m]

        def weights(h):
            b, r = self.B[h % 2], h % 2
            self.mm(b.ap[:, 0:256], LOW, SP[:, r, 0:256], False, True, [*mids[h], cst_in], loose=True)
            self.mm(b.ap[:, 128:256], ONES, SP[:, r, 256:384], False, True, loose=True)
            self.mm(b.ap[:, 256:384], LOW, SP[:, r, 256:384], False, True, loose=True)
            self.mm(b.ap[:, 0:128], self.IDENT, NMASK, False, True, loose=True)
            t = self.mm(b.ap[:, 256:384], self.IDENT, NMASK, False, True, loose=True)
            sp_free[r] = [t]
            ats[h] = self.act(AT[:, r, :], b.ap[:, 0:384], ACT.Exp, [t, *at_free[r]])
            b.free = [ats[h]]

        def values(h):
            b, r = self.B[2 + h % 2], h % 2
            col = slice(h * 64, h * 64 + 64)
            self.mm(b.ap[:, 0:64], AT[:, r, 0:128], v[:, 0, col], True, True, [ats[h], *b.free])
            self.mm(b.ap[:, 64:128], AT[:, r, 128:256], v[:, 0, col], True, False)
            t = self.mm(b.ap[:, 64:128], AT[:, r, 256:384], v[:, 1, col], False, True)
            at_free[r] = [t]
            b.free = [self.cp(O[:, :, col], b.ap[:, 0:128].rearrange("p (b d) -> p b d", b=2), [t])]
            ends[h] = b.free[0]

        for i in range(14):
            if i < 12:
                scores(i)
            if 1 <= i <= 12:
                weights(i - 1)
            if i >= 2:
                values(i - 2)
        end = self.mem_attention(1, ar, qmT, O, [Q.last["pe"]])
        t = self.project_out("bwo", 0, O, [ends[10], ends[11], *end])
        return self.deepnorm(ar, gb, gb_in, t)

    def route(self, S, S2, CD, C2, ar, s_in):
        v3 = lambda x, a, b: x.rearrange("p (a b) -> p a b", a=a)
        for blk in range(2):
            base = ar.at
            TV, TI, TF = v3(ar(256), 16, 16), ar(256), v3(ar(256), 16, 16)
            TIu = v3(TI.bitcast(U32), 16, 16)
            S1, S2v = v3(S[blk], 16, 128), v3(S2, 16, 128)
            BV, BP, BI, BJ = v3(ar(128), 8, 16), ar(128), ar(128), ar(128)
            GW, AI, BB = ar(128), ar(128), ar(128)
            BPu, BIu, BJu = (v3(x.bitcast(U32), 8, 16) for x in (BP, BI, BJ))
            IF, JF, sc = ar(128), ar(128), ar(24)
            ar.at = base

            def top(n, tv, ti, s1, s2, after, cost):
                m1, x1, r1, m2, x2 = {}, {}, {}, {}, {}
                for k in range(n):
                    m1[k] = self.Q.op("dve", self.max8(tv[:, k, 0:8], s1[:, k, :]), after)
                    yield cost
                for k in range(n):
                    x1[k] = self.Q.op("dve", self.idx8(ti[:, k, 0:8], tv[:, k, 0:8], s1[:, k, :]), [m1[k], *after])
                    yield cost
                for k in range(n):
                    r1[k] = self.Q.op("dve", self.rep8(s2[:, k, :], tv[:, k, 0:8], s1[:, k, :]), [m1[k], *after])
                    yield cost
                for k in range(n):
                    m2[k] = self.Q.op("dve", self.max8(tv[:, k, 8:16], s2[:, k, :]), [r1[k]])
                    yield cost
                for k in range(n):
                    x2[k] = self.Q.op("dve", self.idx8(ti[:, k, 8:16], tv[:, k, 8:16], s2[:, k, :]), [m2[k], r1[k]])
                    yield cost
                self.topped = [x1[n - 1], m2[n - 1], x2[n - 1]]

            prev = [self.Q.last["dve"], self.Q.last["act"]]
            if blk:
                prev += self.routed
            yield from top(16, TV, TIu, S1, S2v, [*s_in[0], *s_in[1], *prev], 1)
            done = self.topped
            f = self.cp(TF, TIu, done)
            tv4 = TV.rearrange("p (h a) n -> p h a n", a=2)
            tf4 = TF.rearrange("p (h a) n -> p h a n", a=2)
            cd4 = CD.rearrange("p (h i j) -> p h i j", h=8, i=16)
            for h in range(0, 8, 4):
                c = self.tt(cd4[:, h:h + 4], tv4[:, h:h + 4, 0, :].unsqueeze(3).to_broadcast([P, 4, 16, 16]),
                            tv4[:, h:h + 4, 1, :].unsqueeze(2).to_broadcast([P, 4, 16, 16]), ALU.add, done)
                yield 5
            yield from top(8, BV, BPu, v3(CD, 8, 256), v3(C2, 8, 256), [c], 1.7)
            done2 = self.topped
            e1 = self.tt(v3(GW, 8, 16), BV, BV[:, :, 0:1].to_broadcast([P, 8, 16]), ALU.subtract, done2)
            e2 = self.act(GW, GW, ACT.Exp, [e1])
            i1 = self.ts(BIu, BPu, 4, None, ALU.logical_shift_right, None, done2)
            j1 = self.ts(BJu, BPu, 15, None, ALU.bitwise_and, None, done2)
            i2 = self.cp(v3(IF, 8, 16), BIu, [i1])
            j2 = self.cp(v3(JF, 8, 16), BJu, [j1])
            yield 2
            e3 = self.red(sc[:, 0:8], v3(GW, 8, 16), ALU.add, [e2])
            e4 = self.rcp(sc[:, 8:16], sc[:, 0:8], [e3])
            e5 = self.tt(v3(GW, 8, 16), v3(GW, 8, 16), sc[:, 8:16].unsqueeze(2).to_broadcast([P, 8, 16]), ALU.mult, [e4, e3])
            yield 1
            ends = [e5]
            prior = [c, *done2]
            for src, ready, dst, half, buf, eng in ((JF, j2, BB, 1, C2, "pool"), (IF, i2, AI, 0, CD, "dve")):
                cost = 5 if eng == "dve" else 0.5
                b4 = buf.rearrange("p (h k i) -> p h k i", h=8, k=16)
                for h in range(0, 8, 4):
                    hk = slice(16 * h, 16 * h + 64)
                    eq = self.tt(v3(buf, 128, 16)[:, hk, :], src[:, hk].unsqueeze(2).to_broadcast([P, 64, 16]),
                                 self.IOTA[:, 0:16].unsqueeze(1).to_broadcast([P, 64, 16]), ALU.is_equal, [ready, *prior])
                    yield 5
                    mu = self.tt(b4[:, h:h + 4], b4[:, h:h + 4], tf4[:, h:h + 4, half, :].unsqueeze(2).to_broadcast([P, 4, 16, 16]),
                                 ALU.mult, [eq, f], eng)
                    yield cost
                    if eng == "dve":
                        ends.append(self.red(dst[:, hk], v3(buf, 128, 16)[:, hk, :], ALU.add, [mu]))
                        yield cost
                if eng == "pool":
                    late = (dst, buf, mu)
            dst, buf, mu = late
            for h in range(0, 8, 4):
                hk = slice(16 * h, 16 * h + 64)
                ends.append(self.red(dst[:, hk], v3(buf, 128, 16)[:, hk, :], ALU.add, [mu]))
                yield 5
            b = self.B[4]
            for k, x in enumerate((AI, BB, GW)):
                t = self.tr(b.ap[:, k * 128:k * 128 + 128], x, [*ends, *b.free])
            z = self.cp(self.ABG[:, :, blk * 128:blk * 128 + 128], v3(b.ap[:, 0:384], 3, 128), [t])
            b.free = [z]
            self.routed = [z, *ends]
            yield 1

    def max8(self, out, in_):
        return lambda e: e.max(out, in_)

    def idx8(self, out, top, in_):
        return lambda e: e.max_index(out, top, in_)

    def rep8(self, out, top, in_):
        return lambda e: e.match_replace(out, top, in_, LOWEST)

    def gates(self, part, G, got):
        iota = self.IOTA[:, part * GP:part * GP + GP].unsqueeze(1).to_broadcast([P, 4, GP])
        made = {}
        for step in range(65):
            n0 = 4 * step
            if step < 64:
                s0 = 4 * (step % 2)
                old = self.oh_free[step % 2]
                one = [self.ts(self.OHA[:, s0 + k, :], self.IOTA, self.ABG[:, 0, n0 + k:n0 + k + 1], self.ABG[:, 2, n0 + k:n0 + k + 1],
                               ALU.is_equal, ALU.mult, [*self.routed, *old]) for k in range(4)]
                one.append(self.tt(self.OHB[:, s0:s0 + 4, :], iota, self.ABG[:, 1, n0:n0 + 4].unsqueeze(2).to_broadcast([P, 4, GP]),
                                   ALU.is_equal, [*self.routed, *old]))
                made[step] = one
            if step:
                m0 = n0 - 4
                s0 = m0 % 8
                bank = self.B[4 + (m0 // 8) % 2]
                for k in range(4):
                    w = self.mm(bank.ap[:, (s0 + k) * GP:(s0 + k) * GP + GP], self.OHA[:, s0 + k, :], self.OHB[:, s0 + k, :], True, True,
                                [*made[step - 1], *bank.free])
                self.oh_free[(step - 1) % 2] = [w]
                if s0 == 4:
                    g = G[:, part * GP:part * GP + GP, m0 - 4:m0 + 4].rearrange("p i n -> p n i")
                    m = self.tt(g, g, bank.ap[:, :].rearrange("p (n i) -> p n i", n=8), ALU.mult, [w, *got()])
                    bank.free = [m]
                    self.gated[part] = m
            yield 1

    def peer(self, layer, xt):
        G = self.BIG[:, :].rearrange("p (g n) -> p g n", g=128)
        ar = Arena(self.BIG, PARTS and 32768 // 2)
        q0 = ar.at
        qT = ar(4096).rearrange("p (c n) -> p c n", c=16)
        SK = ar(2048)
        S = [ar(2048), ar(2048)]
        sk_in = self.load(SK, self.small["sk"][layer])
        qt = []
        aft = xt
        for k in range(16):
            b = self.B[4 + k % 4]
            t = self.cols_unit(("wq", layer, k), b.ap[:, 0:256], [*aft, *b.free])
            aft = []
            qt.append(self.cp(qT[:, k, :], b.ap[:, 0:256], [t], "act"))
            b.free = [qt[-1]]
        s_in = []
        for blk in range(2):
            s_in.append([])
            for c in range(4):
                b = self.B[c]
                for k in range(4):
                    hp = 4 * c + k
                    t = self.mm(b.ap[:, k * 128:k * 128 + 128], qT[:, hp, blk * 128:blk * 128 + 128],
                                SK[:, hp * 128:hp * 128 + 128], True, True, [qt[hp], sk_in, *b.free])
                b.free = [self.cp(S[blk][:, c * 512:c * 512 + 512], b.ap[:, :], [t], "dve" if c % 2 else "act")]
                s_in[blk] += b.free
        work = self.route(S, SK, self.BIG[:, q0:q0 + 2048], self.BIG[:, q0 + 2048:q0 + 4096], ar, s_in)

        def drive(gen, n):
            while n > 0:
                try:
                    n -= next(gen) or 1
                except StopIteration:
                    return False
            return True

        acts = {}
        self.gated = {}
        self.oh_free = [[], []]

        def up(g, gen, n, after=()):
            b = self.B[6 + (g // 2) % 2]
            o = (g % 2) * 256
            t = self.cols_unit(("u", layer, g), b.ap[:, o:o + 256], b.free if g % 2 == 0 else [])
            if g % 2:
                acts[g] = self.act(G[:, g - 1:g + 1, :], b.ap[:, :].rearrange("p (a n) -> p a n", a=2), ACT.Gelu, [t, *after])
                b.free = [acts[g]]
            drive(gen, n)

        for g in range(GP):
            up(g, work, 7)
        drive(work, 10 ** 6)
        work = self.gates(0, G, lambda: [acts[GP - 1]])
        over = [*self.routed, self.Q.last["pe"]]
        self.share = 2
        for g in range(GP, 128):
            up(g, work, 1, over if g == GP + 1 else [])
        drive(work, 10 ** 6)
        work = self.gates(1, G, lambda: [acts[127]])
        gfree = [[], []]

        def split_g(g, part):
            r = g % 2
            h = self.cp(self.GH[:, r, :], G[:, g, :], [self.gated[part], *gfree[r]], "act")
            l = self.tt(self.GL[:, r, :], G[:, g, :], self.GH[:, r, :].bitcast(F32), ALU.subtract,
                        [h, self.gated[part], *gfree[r]])
            return [h, l]

        def down(g, ready, first, last):
            r = g % 2
            t = self.depth_unit(("v", layer, g), self.GH[:, r, :], self.GL[:, r, :], first, last, ready)
            gfree[r] = [t]
            return t

        free = [f for b in self.B[0:4] for f in b.free]
        for part in range(2):
            lo = part * GP
            nxt = split_g(lo, part)
            for g in range(lo, lo + GP):
                ready = nxt
                if g + 1 < lo + GP:
                    nxt = split_g(g + 1, part)
                t = down(g, [*ready, *free], g == 0, g == 127)
                free = []
                if part == 0:
                    drive(work, 1)
            if part == 0:
                drive(work, 10 ** 6)
                self.share = 4
                la = Arena(self.BIG, 0, 32768 // 2)
                gb, gb_in = self.load_gb(la, 2 * layer + 1, [t, nxt[0], nxt[1]])
        return self.deepnorm(la, gb, gb_in, t)

    def ffn(self, layer, which):
        ar = Arena(self.BIG)
        XN = ar(2048).rearrange("p (b n) -> p b n", b=2)
        sc = ar(16)
        xn = self.rms_rows(XN, sc, [])
        k = layer * 3 + (0 if which == 1 else 2)
        xt = self.to_xt(XN, xn, self.COLS[:, 8 * k:8 * k + 8])
        SG = ar(2 * 256).rearrange("p (r n) -> p r n", r=2)
        HID = ar(2 * 256).rearrange("p (r n) -> p r n", r=2)
        gfree, hfree, sfree = [[], []], [[], []], [[], []]
        ready = {}
        n = 22
        aft = xt
        for f in range(n + 1):
            if f < n:
                b, r = self.B[4 + f % 4], f % 2
                t1 = self.cols_unit(("fg", layer, which, f), b.ap[:, 0:256], [*aft, *b.free])
                aft = []
                t2 = self.cols_unit(("fu", layer, which, f), b.ap[:, 256:512], [])
                s = self.act(SG[:, r, :], b.ap[:, 0:256], ACT.Silu, [t1, t2, *sfree[r]])
                h = self.tt(HID[:, r, :], SG[:, r, :], b.ap[:, 256:512], ALU.mult, [s, t2, *hfree[r]])
                b.free = [s, h]
                sfree[r] = [h]
                gh = self.cp(self.GH[:, r, :], HID[:, r, :], [h, *gfree[r]], "act")
                gl = self.tt(self.GL[:, r, :], HID[:, r, :], self.GH[:, r, :].bitcast(F32), ALU.subtract, [gh, h, *gfree[r]])
                hfree[r] = [gh, gl]
                ready[f] = [gh, gl]
            if f >= 1:
                r = (f - 1) % 2
                free = [x for bb in self.B[0:4] for x in bb.free] if f == 1 else []
                t = self.depth_unit(("fd", layer, which, f - 1), self.GH[:, r, :], self.GL[:, r, :], f == 1, f == n,
                                    [*ready[f - 1], *free])
                gfree[r] = [t]
        return self.add_to_h(0.5, t)

    def add_to_h(self, scale, t):
        toks = []
        for blk in range(2):
            for half in range(2):
                b = self.B[blk * 2 + half]
                x = self.H[:, blk, 512 * half:512 * half + 512]
                z = self.stt(x, b.ap[:, :], scale, x, ALU.mult, ALU.add, [t])
                b.free = [z]
                toks.append(z)
        return toks

    def rope(self, X, heads, x1, x2, cos, sin, tmp, after, eng):
        half = cos.shape[2]
        shape = [P, 2, heads, half]
        a, b = X[:, :, :, x1:x1 + half], X[:, :, :, x2:x2 + half]
        c, s = cos.unsqueeze(2).to_broadcast(shape), sin.unsqueeze(2).to_broadcast(shape)
        n = 2 * heads * half
        t = [tmp(n).rearrange("p (b h d) -> p b h d", b=2, h=heads) for _ in range(4)]
        m = [self.tt(t[0], a, c, ALU.mult, after, eng), self.tt(t[1], b, s, ALU.mult, after, eng),
             self.tt(t[2], a, s, ALU.mult, after, eng), self.tt(t[3], b, c, ALU.mult, after, eng)]
        return [self.tt(a, t[0], t[1], ALU.subtract, m, eng), self.tt(b, t[2], t[3], ALU.add, m, eng)]

    def mix(self, layer):
        ar = Arena(self.BIG)
        XN = ar(2048).rearrange("p (b n) -> p b n", b=2)
        sc = ar(16)
        NAB = ar(2048).rearrange("p (b h n) -> p b h n", b=2, h=4)
        nab_in = self.load(self.BIG[:, ar.at - 2048:ar.at], self.small["na_bias"][layer])
        MC = ar(256 + 512 + 176)
        mc_in = self.load(MC, self.small["mix_c"])
        NAM = MC[:, 0:256]
        LOGC = MC[:, 256:768].rearrange("p (b n) -> p b n", b=2)
        RT = MC[:, 768:944].rearrange("p (b n) -> p b n", b=2)
        GAIN = ar(1920)
        gn_in = self.load(GAIN, self.small["qk_gain"][layer].unsqueeze(0).to_broadcast([P, 1920]))
        DG = ar(64)
        dg_in = self.load(DG, self.small["d_gain"][layer].unsqueeze(0).to_broadcast([P, 64]))
        LV = ar(128)
        lv_in = self.load(LV, self.small["lam"][layer].unsqueeze(0).to_broadcast([P, 128]))
        X = ar(2 * 2816).rearrange("p (b n) -> p b n", b=2)
        SQ = ar(2 * 1920).rearrange("p (b n) -> p b n", b=2)
        ss = ar(3 * 76).rearrange("p (k n) -> p k n", k=3)
        xn = self.rms_rows(XN, sc, [])
        k = layer * 3 + 1
        xt = self.to_xt(XN, xn, self.COLS[:, 8 * k:8 * k + 8])
        init = 0.8 - 0.6 * math.exp(-0.3 * layer)
        nb = self.tt(NAB.rearrange("p b h n -> p (b h) n"), NAB.rearrange("p b h n -> p (b h) n"),
                     NAM.unsqueeze(1).to_broadcast([P, 8, 256]), ALU.add, [nab_in, mc_in], "pool")
        gs = []
        for lo, hi, s in ((0, 256, 0.125), (512, 768, 0.125), (1024, 1280, 0.125), (1408, 1664, 32 ** -0.5)):
            gs.append(self.ts(GAIN[:, lo:hi], GAIN[:, lo:hi], s, None, ALU.mult, None, [gn_in], "pool"))
        gs.append(gn_in)
        dg = self.ts(DG, DG, 1.0 - init, None, ALU.mult, None, [dg_in], "pool")
        lm = ar(8)
        lt = ar(64)
        l0 = self.tt(lt, LV[:, 0:64], LV[:, 64:128], ALU.mult, [lv_in])
        l1 = self.red(lm[:, 0:2], lt.rearrange("p (a n) -> p a n", a=2), ALU.add, [l0])
        l2 = self.act(lm[:, 2:4], lm[:, 0:2], ACT.Exp, [l1])
        l3 = self.tt(lm[:, 4:5], lm[:, 3:4], lm[:, 2:3], ALU.subtract, [l2])
        l4 = self.ts(lm[:, 5:6], lm[:, 4:5], -init, None, ALU.add, None, [l3])
        NLAM = lm[:, 5:6]
        xs, sq = [], []
        aft = xt
        for c in range(6):
            width = 512 if c < 5 else 256
            outs = [self.B[2 * (c % 2)], self.B[2 * (c % 2) + 1]]
            t = self.rows_block([("win", layer, c, k2) for k2 in range(4 if c < 5 else 2)], [b.ap[:, 0:width] for b in outs], width,
                                [*aft, *outs[0].free, *outs[1].free])
            aft = []
            for blk in range(2):
                cols = slice(c * 512, c * 512 + width)
                x = self.cp(X[:, blk, cols], outs[blk].ap[:, 0:width], [t], "act")
                outs[blk].free = [x]
                xs.append(x)
                if c < 4:
                    w = min(512, 1920 - c * 512)
                    sq.append(self.act(SQ[:, blk, c * 512:c * 512 + w], outs[blk].ap[:, 0:w], ACT.Square, [t]))
                    outs[blk].free.append(sq[-1])
        s64, s32 = ss[:, 0, 0:44].rearrange("p (b h) -> p b h", b=2), ss[:, 0, 44:76].rearrange("p (b h) -> p b h", b=2)
        rd = []
        for blk in range(2):
            rd.append(self.red(s64[:, blk, :], SQ[:, blk, 0:1408].rearrange("p (h d) -> p h d", d=64), ALU.add, sq))
            rd.append(self.red(s32[:, blk, :], SQ[:, blk, 1408:1920].rearrange("p (h d) -> p h d", d=32), ALU.add, sq))
        q1 = self.act(ss[:, 1, 0:44], ss[:, 0, 0:44], ACT.Sqrt, rd, scale=1.0 / 64, bias=self.EPS6)
        q2 = self.act(ss[:, 1, 44:76], ss[:, 0, 44:76], ACT.Sqrt, rd, scale=1.0 / 32, bias=self.EPS6)
        rr = self.rcp(ss[:, 2, :], ss[:, 1, :], [q1, q2])
        r64, r32 = ss[:, 2, 0:44].rearrange("p (b h) -> p b h", b=2), ss[:, 2, 44:76].rearrange("p (b h) -> p b h", b=2)
        nm = []
        for blk in range(2):
            x64 = X[:, blk, 0:1408].rearrange("p (h d) -> p h d", d=64)
            x32 = X[:, blk, 1408:1920].rearrange("p (h d) -> p h d", d=32)
            a = self.tt(x64, x64, r64[:, blk, :].unsqueeze(2).to_broadcast([P, 22, 64]), ALU.mult, [rr, *xs, *sq])
            b = self.tt(x32, x32, r32[:, blk, :].unsqueeze(2).to_broadcast([P, 16, 32]), ALU.mult, [rr, *xs, *sq])
            nm.append(self.tt(X[:, blk, 0:1920], X[:, blk, 0:1920], GAIN, ALU.mult, [a, b, *gs]))
        tmp = Arena(self.BIG, ar.at)
        rp = []
        rp += self.rope(X[:, :, 512:1024].rearrange("p b (h d) -> p b h d", d=64), 8, 0, 8, RT[:, :, 8:16], RT[:, :, 16:24], tmp,
                        [*nm, mc_in], "dve")
        gx = X[:, :, 1024:1408].rearrange("p b (h d) -> p b h d", d=64)
        rp += self.rope(gx, 6, 0, 16, RT[:, :, 24:40], RT[:, :, 40:56], tmp, [*nm, mc_in], "pool")
        rp += self.rope(gx, 6, 32, 48, RT[:, :, 56:72], RT[:, :, 72:88], tmp, [*nm, mc_in], "dve")
        rp += self.rope(X[:, :, 1408:1920].rearrange("p b (h d) -> p b h d", d=32), 16, 0, 4, RT[:, :, 0:4], RT[:, :, 4:8], tmp,
                        [*nm, mc_in], "dve")
        QK = ar(15 * 256).rearrange("p (c n) -> p c n", c=15)
        ar.at = max(ar.at, tmp.at)
        qk = []
        for g in range(8):
            b = self.B[4 + g % 4]
            for k2 in range(2 if g < 7 else 1):
                for blk in range(2):
                    c = 2 * g + k2
                    t = self.tr(b.ap[:, k2 * 256 + blk * 128:k2 * 256 + blk * 128 + 128], X[:, blk, c * 128:c * 128 + 128],
                                [*nm, *rp, *b.free])
            w = 2 if g < 7 else 1
            q = self.cp(QK[:, 2 * g:2 * g + w, :], b.ap[:, 0:256 * w].rearrange("p (a n) -> p a n", a=w), [t, *rp],
                        "act" if g % 2 else "dve")
            b.free = [q]
            qk.append(q)
        O = XN
        o_free = [self.Q.last["pe"]]

        def put(col):
            return lambda ps, r, aft2: self.tt(O[:, :, col:col + 64], ps, r, ALU.mult, [*aft2, *o_free])

        D1 = ar(128).rearrange("p (b d) -> p b d", b=2)
        d1_free = []

        def put_minus(col, d1_free):
            def go(ps, r, aft2):
                x = self.tt(D1, ps, r, ALU.mult, [*aft2, *d1_free])
                y = self.stt(O[:, :, col:col + 64], D1, NLAM, O[:, :, col:col + 64], ALU.mult, ALU.add, [x, l4])
                d1_free[:] = [y]
                return y
            return go

        def vcols(lo):
            return [X[:, s, lo:lo + 64] for s in range(2)]

        heads = []
        base = dict(after=[*qk, *xs], bias=None, bias_after=[])
        for h in range(4):
            o = slice((h % 2) * 64, (h % 2) * 64 + 64)
            heads.append(dict(base, q=QK[o, h // 2, :], k=QK[o, 2 + h // 2, :], v=vcols(1920 + 64 * h), bias=NAB[:, :, h, :],
                              bias_after=[nb], finish=put(64 * h)))
            heads.append(dict(base, q=QK[o, 4 + h // 2, :], k=QK[o, 6 + h // 2, :], v=vcols(2560 + 64 * h), bias=LOGC,
                              bias_after=[mc_in], finish=put(768 + 64 * h)))
            kv = h // 2
            o = slice(kv * 64, kv * 64 + 64)
            heads.append(dict(base, q=QK[o, 8 + h % 2, :], k=QK[o, 10, :], v=vcols(2432 + 64 * kv), finish=put(512 + 64 * h)))
            for i in range(2):
                sub = 2 * h + i
                o = slice((sub % 4) * 32, (sub % 4) * 32 + 32)
                heads.append(dict(base, q=QK[o, 11 + sub // 4, :], k=QK[o, 13 + sub // 4, :], v=vcols(2176 + 64 * h),
                                  finish=put_minus(256 + 64 * h, d1_free) if i else put(256 + 64 * h)))
        end = self.attention(heads, ar)
        OD = O[:, :, 256:512].rearrange("p b (h d) -> p b h d", d=64)
        sq4 = SQ[:, :, 0:256].rearrange("p b (h d) -> p b h d", d=64)
        d0 = self.tt(sq4, OD, OD, ALU.mult, [*end, *rd])
        d1 = self.red(ss[:, 0, 0:8].rearrange("p (b h) -> p b h", b=2), sq4, ALU.add, [d0])
        d2 = self.act(ss[:, 1, 0:8], ss[:, 0, 0:8], ACT.Sqrt, [d1], scale=1.0 / 64, bias=self.EPS6)
        d3 = self.rcp(ss[:, 2, 0:8], ss[:, 1, 0:8], [d2])
        d4 = self.tt(OD, OD, ss[:, 2, 0:8].rearrange("p (b h) -> p b h", b=2).unsqueeze(3).to_broadcast([P, 2, 4, 64]), ALU.mult,
                     [d3, d0])
        od8 = O[:, :, 256:512].rearrange("p b (h d) -> p b h d", d=64)
        d5 = []
        for blk in range(2):
            d5.append(self.tt(od8[:, blk], od8[:, blk], DG.unsqueeze(1).to_broadcast([P, 4, 64]), ALU.mult, [d4, dg]))
        t = self.project_out("w2o", layer, O, [*end, *d5])
        return self.add_to_h(1.0, t)

    def build(self):
        sm = self.small
        ar = Arena(self.BIG, 32768 - 2048)
        xT = ar(2048).rearrange("p (c n) -> p c n", c=8)
        x_in = self.load(xT, sm["xT"])
        c_in = self.load(self.CST[:, :], sm["cst"])
        self.h_in = self.load(self.H[:, :, :], sm["x"])
        toks = self.split_xt(xT, [x_in])
        for e in ("pe", "act", "dve", "pool"):
            self.Q.fence[e] = [c_in]
        for _ in range(NHALF):
            self.split_next()
        stages = [lambda: self.gla_mixer(toks), lambda: self.peer(0, self.turned()), lambda: self.sb_mixer(self.turned()),
                  lambda: self.peer(1, self.turned())]
        for layer in range(DEPTH):
            stages += [self.ffn_stage(layer, 1), self.mix_stage(layer), self.ffn_stage(layer, 2)]
        for n, stage in enumerate(stages[0:self.upto]):
            if n:
                self.Q.phase()
            toks = stage()
        out = Landed(self.sem("s_out"), 16)
        self.Q.dma("act", lambda e: e.dma_start(self.out, self.H[:, :, :]), out, toks)
        self.final = out
        assert self.n_taken == 2 * self.n_units, (self.n_taken, self.n_units)

    def ffn_stage(self, layer, which):
        return lambda: self.ffn(layer, which)

    def mix_stage(self, layer):
        return lambda: self.mix(layer)

    def turned(self):
        return self.to_xt(self.H, [])

    def emit(self, w):
        self.stream_dmas(w)
        self.Q.count(self.sems)
        nc, Q, sems = self.nc, self.Q, self.sems
        block = self.ctx.enter_context(nc.Block())

        @block.sync
        def _(e):
            Q.emit("sp", e, sems)

        @block.gpsimd
        def _(e):
            Q.emit("pool", e, sems)

        @block.vector
        def _(e):
            Q.emit("dve", e, sems)

        @block.tensor
        def _(e):
            Q.emit("pe", e, sems)

        @block.scalar
        def _(e):
            Q.emit("act", e, sems)
            e.wait_ge(self.final.sem, self.final.val)


UNITS = [33, 272, 32, 272, 66, 30, 66, 66, 30, 66]


def _column_units(np, w):
    n = w.shape[1] // 128
    return w.reshape(8, 128, n, 128).transpose(2, 1, 0, 3).reshape(n, 128, 1024)


def _row_units(np, w):
    n = w.shape[1] // 512
    out = w[:, 0:512 * n].reshape(4, 2, 128, n, 512).transpose(3, 0, 2, 1, 4).reshape(n, 4, 128, 1024)
    rest = w[:, 512 * n:]
    tail = rest.reshape(2, 4, 128, 256).transpose(0, 2, 1, 3).reshape(2, 128, 1024) if rest.shape[1] else None
    return out, tail


def _layout(np, x, keys):
    f = {}
    need = {k[0] for k in keys}
    aw = x["a_w_in"][0]
    if "aq" in need:
        for name, lo, n in (("aq", 0, 384), ("ak", 384, 384), ("aqm", 2320, 256)):
            u = _column_units(np, aw[:, lo:lo + n])
            for k in range(len(u)):
                f[(name, k)] = u[k]
        glr = np.zeros((1024, 128), np.float32)
        glr[:, 0:16] = aw[:, 2304:2320]
        f[("glr", 0)] = _column_units(np, glr)[0]
        u, _ = _row_units(np, aw[:, 768:2304])
        for c in range(3):
            for k in range(4):
                f[("avr", c, k)] = u[c, k]
    for layer, name in ((0, "a"), (1, "b")):
        w = x[name + "_w_mem_kv"][0]
        u = _column_units(np, w[:, 0:256])
        _, tail = _row_units(np, w[:, 256:512])
        for k in range(2):
            f[("km", layer, k)], f[("vm", layer, k)] = u[k], tail[k]
        for c in range(8):
            f[(name + "wo", 0, c)] = x[name + "_w_out"][0][c * 128:c * 128 + 128]
    if "bk" in need:
        kv, bw = x["sb_w_kv"], x["b_w_in"][0]
        for name, w in (("bk", kv[:, 0:768]), ("bq", bw[:, 0:768]), ("bqm", bw[:, 768:1024])):
            u = _column_units(np, w)
            for k in range(len(u)):
                f[(name, k)] = u[k]
        u, tail = _row_units(np, kv[:, 768:1536])
        for k in range(4):
            f[("bv", 0, k)] = u[0, k]
        for k in range(2):
            f[("bv", 1, k)] = tail[k]
    for layer in range(DEPTH):
        if ("wq", layer, 0) in keys:
            u = _column_units(np, x["peer_w_q"][layer])
            for k in range(16):
                f[("wq", layer, k)] = u[k]
            pu = x["peer_u"][layer].reshape(128, 128, 8, 128)
            pv = x["peer_v"][layer].reshape(128, 128, 1024)
            for g in range(128):
                f[("u", layer, g)] = pu[:, g].transpose(2, 1, 0).reshape(128, 1024)
                f[("v", layer, g)] = pv[:, g]
        for which in (1, 2):
            if ("fg", layer, which, 0) in keys:
                ug = _column_units(np, x[f"ffn{which}_w_gate_2"][layer])
                uu = _column_units(np, x[f"ffn{which}_w_up_2"][layer])
                for k in range(22):
                    f[("fg", layer, which, k)], f[("fu", layer, which, k)] = ug[k], uu[k]
                    f[("fd", layer, which, k)] = x[f"ffn{which}_w_down_2"][layer][k * 128:k * 128 + 128]
        if ("win", layer, 0, 0) in keys:
            w = x["w_in_2"][layer]
            na, df, gq, dl = w[:, 0:768], w[:, 768:1536], w[:, 1536:2048], w[:, 2048:2816]
            gqq = gq[:, 0:256].reshape(1024, 4, 64)[:, [0, 2, 1, 3]].reshape(1024, 256)
            w = np.concatenate([na[:, 0:512], dl[:, 0:512], gqq, gq[:, 256:384], df[:, 0:512], na[:, 512:768], df[:, 512:768],
                                gq[:, 384:512], dl[:, 512:768]], axis=1)
            u, tail = _row_units(np, w)
            for c in range(5):
                for k in range(4):
                    f[("win", layer, c, k)] = u[c, k]
            for k in range(2):
                f[("win", layer, 5, k)] = tail[k]
            for c in range(8):
                f[("w2o", layer, c)] = x["w_out_2"][layer][c * 128:c * 128 + 128]
    out = np.empty((len(keys), 128, 1024), np.float32)
    for n, k in enumerate(keys):
        out[n] = f[k]
    return out


def _constants(np):
    i = np.arange(128)
    f32 = np.float32
    cst = np.zeros((128, 264), f32)
    cst[:, 0:128] = np.eye(128)
    cst[:, 128:256] = i[None, :]
    cst[:, 256], cst[:, 257], cst[:, 258] = 1e-5, 1e-6, 1.0
    causal = ((i[:, None] <= i[None, :]) & (i[:, None] // 64 == i[None, :] // 64)).astype(f32)
    gla = np.concatenate([causal, causal / 16.0], axis=1)
    low = -(i[:, None] >= i[None, :]).astype(f32)
    strict = (i[:, None] < i[None, :]).astype(f32)
    sb = np.concatenate([low, -np.ones((128, 128), f32), strict, np.where(strict > 0, 0.0, NEG).astype(f32)], axis=1)
    cols = np.arange(64)
    first = np.clip(cols - 8, 0, 48)
    win = (cols[None, :] >= first[:, None]) & (cols[None, :] < first[:, None] + 16)
    nam = np.where(np.tile(win, (2, 4)), 0.0, NEG).astype(f32)
    d = np.arange(256)[:, None] - np.arange(256)[None, :]
    count = (np.abs(d) <= 64).astype(int) + (d % 4 == 0) + (d % 16 == 0)
    logc = np.where(count > 0, np.log(np.maximum(count, 1)), NEG).astype(f32).reshape(2, 128, 256).transpose(1, 0, 2)

    def table(pos, dim, theta):
        inv = (f32(1.0) / (f32(theta) ** (np.arange(0, dim, 2, dtype=f32) / f32(dim)))).astype(f32)
        ang = pos.astype(f32)[:, None] * inv[None, :]
        return [np.cos(ang).astype(f32), np.sin(ang).astype(f32)]

    pos = np.arange(256)
    rt = np.concatenate(table(pos, 8, 500000.0) + table(pos, 16, 500000.0) + table(pos // 64, 32, 10000.0)
                        + table(pos % 64, 32, 10000.0), axis=1)
    rt = rt.reshape(2, 128, 88).transpose(1, 0, 2).reshape(128, 176)
    mix = np.concatenate([nam, logc.reshape(128, 512), rt], axis=1).astype(f32)
    return cst, gla.astype(f32), sb.astype(f32), mix


def _small(np, x):
    cst, gla, sb, mix = _constants(np)
    xx, mem = x["x"][0], x["mem"][0]
    cols = [x[n][layer].reshape(8, 128).T for layer in range(DEPTH) for n in ("ffn1_norm_2", "mix_norm_2", "ffn2_norm_2")]
    s = {"cst": np.concatenate([cst] + cols, axis=1), "gla_c": gla, "sb_c": sb, "mix_c": mix}
    s["x"] = xx.reshape(2, 128, 1024).transpose(1, 0, 2)
    s["xT"] = xx.reshape(256, 8, 128).transpose(2, 1, 0)
    s["memT"] = mem.reshape(256, 8, 128).transpose(2, 1, 0)
    s["ln"] = np.stack([np.stack([x["ln_g"][a, b], x["ln_b"][a, b]]) for a in range(2) for b in range(2)])
    s["head_g"] = x["a_head_g"].reshape(1, 768)
    s["wg2"] = np.concatenate([x["a_w_gate2"][0], x["a_b_gate"]], axis=0)
    s["sk"] = x["peer_subkeys"].reshape(2, 16, 128, 128).transpose(0, 3, 1, 2).reshape(2, 128, 2048)
    gains = []
    for layer in range(DEPTH):
        g = [(n, r) for n, r in (("na_q", 4), ("na_k", 4), ("dil_q", 4), ("dil_k", 4), ("gqa_q", 4), ("gqa_k", 2), ("diff_q", 8),
                                 ("diff_k", 8))]
        gains.append(np.concatenate([np.tile(x[n + "_norm_2"][layer], r) for n, r in g]))
    s["qk_gain"] = np.stack(gains)
    s["d_gain"] = x["diff_out_norm_2"]
    s["lam"] = np.concatenate([x[f"diff_lambda_{n}_2"] for n in ("q1", "q2", "k1", "k2")], axis=1)
    q, key = np.arange(256), np.arange(256)
    ro = key[None, :] // 64 - q[:, None] // 64 + 7
    co = np.clip(key[None, :] % 64 - q[:, None] % 64 + 15, 0, 30)
    nab = x["na_rel_bias_2"][:, :, ro, co]
    s["na_bias"] = nab.reshape(2, 4, 2, 128, 256).transpose(0, 3, 2, 1, 4).reshape(2, 128, 2048)
    return {k: np.ascontiguousarray(v) for k, v in s.items()}


def build_program(nc, shapes, feed, layout, upto=10):
    aps = {k: nc.dram_tensor("in_" + k, shape, F32, kind="ExternalInput").ap() for k, shape in shapes.items()}
    out = nc.dram_tensor("out_0", (256, 1024), F32, kind="ExternalOutput").ap().rearrange("(b p) n -> p b n", b=2)
    with ExitStack() as ctx:
        p = Program(nc, ctx, sum(UNITS[0:upto]), aps, out, upto)
        p.build()
        feed["in_w"] = layout(p.order)
        w = nc.dram_tensor("in_w", (p.n_units, 128, 1024), F32, kind="ExternalInput").ap()
        p.emit(w)


def kernel(**inputs):
    import numpy as np
    import concourse.bacc as bacc
    from concourse.bass_utils import run_bass_kernel_spmd

    nc = bacc.Bacc("TRN2", target_bir_lowering=False, num_devices=1)
    x = {k: np.asarray(v) for k, v in inputs.items()}
    arrays = _small(np, x)
    feed = {"in_" + k: v for k, v in arrays.items()}
    build_program(nc, {k: v.shape for k, v in arrays.items()}, feed, lambda keys: _layout(np, x, keys))
    r = run_bass_kernel_spmd(nc, [feed], core_ids=[0])
    return r.results[0]["out_0"].reshape(1, 256, 1024)
```
